# Optimizing a Trainium2 kernel written in Bass

```python
import jax, jax.numpy as jnp
from jax import lax
import numpy as np

D_MODEL = 2048
BATCH = 1
SEQ = 256
DEPTH = 1

HEAD_DIM = 128
N_HEADS_DIL = 8
N_HEADS_FOX = 8
D_DIL = N_HEADS_DIL * HEAD_DIM
D_FOX = N_HEADS_FOX * HEAD_DIM
DIL_PATTERNS = ((128, 1), (512, 4), (2048, 16))
MAX_WINDOW = 2048
Q_BLOCK = 128
ROPE_THETA = 500000.0
ROPE_DIM = HEAD_DIM // 4
D_FF = 5632
NORM_EPS = 1e-6
IN_SPLITS = (D_DIL, D_DIL, D_DIL, D_FOX, D_FOX, D_FOX, N_HEADS_FOX, D_MODEL, D_MODEL)
IN_COLS = sum(IN_SPLITS)

kernel_name = "hybrid_dilated_fox_gated_macaron"

def rmsnorm(x, g):
    xf = x.astype(jnp.float32)
    y = xf * lax.rsqrt(jnp.mean(xf * xf, axis=-1, keepdims=True) + NORM_EPS)
    return (y * g.astype(jnp.float32)).astype(x.dtype)

def swiglu(x, w_gate, w_up, w_down):
    return (jax.nn.silu(x @ w_gate) * (x @ w_up)) @ w_down

def split_heads(t, n_heads):
    b, s, _ = t.shape
    return t.reshape(b, s, n_heads, HEAD_DIM).transpose(0, 2, 1, 3)

def merge_heads(t):
    b, h, s, d = t.shape
    return t.transpose(0, 2, 1, 3).reshape(b, s, h * d)

def partial_rope(t):
    s = t.shape[2]
    half = ROPE_DIM // 2
    pos = jnp.arange(s, dtype=jnp.float32)
    inv_freq = ROPE_THETA ** (-jnp.arange(0, ROPE_DIM, 2, dtype=jnp.float32) / ROPE_DIM)
    ang = pos[:, None] * inv_freq[None, :]
    cos, sin = jnp.cos(ang), jnp.sin(ang)
    rot = t[..., :ROPE_DIM].astype(jnp.float32)
    x1, x2 = rot[..., :half], rot[..., half:]
    rotated = jnp.concatenate([x1 * cos - x2 * sin, x2 * cos + x1 * sin], axis=-1)
    return jnp.concatenate([rotated.astype(t.dtype), t[..., ROPE_DIM:]], axis=-1)

def dilated_attention(q, k, v):
    b, h, s, dh = q.shape
    n_blocks = s // Q_BLOCK
    pad = ((0, 0), (0, 0), (MAX_WINDOW, 0), (0, 0))
    kp = jnp.pad(k, pad)
    vp = jnp.pad(v, pad)
    qb = q.reshape(b, h, n_blocks, Q_BLOCK, dh).transpose(2, 0, 1, 3, 4)

    def block(args):
        qblk, blk = args
        t0 = blk * Q_BLOCK
        nums, dens, maxs = [], [], []
        for w, d in DIL_PATTERNS:
            length = w + Q_BLOCK
            rows = length // d
            nq = Q_BLOCK // d
            start = t0 + MAX_WINDOW - w
            kr = lax.dynamic_slice_in_dim(kp, start, length, axis=2).reshape(b, h, rows, d, dh)
            vr = lax.dynamic_slice_in_dim(vp, start, length, axis=2).reshape(b, h, rows, d, dh)
            qr = qblk.reshape(b, h, nq, d, dh)
            sc = jnp.einsum('bhicd,bhrcd->bhcir', qr, kr, preferred_element_type=jnp.float32)
            r = jnp.arange(rows)
            ip = jnp.arange(nq)
            cc = jnp.arange(d)
            band = (r[None, :] >= ip[:, None]) & (r[None, :] <= ip[:, None] + w // d)
            valid = (t0 - w + r[None, :] * d + cc[:, None]) >= 0
            mask = band[None, :, :] & valid[:, None, :]
            sc = jnp.where(mask, sc, -jnp.inf)
            m = jnp.max(sc, axis=-1, keepdims=True)
            p = jnp.exp(sc - m)
            den = jnp.sum(p, axis=-1)
            num = jnp.einsum('bhcir,bhrcd->bhicd', p, vr.astype(jnp.float32))
            nums.append(num.reshape(b, h, Q_BLOCK, dh))
            dens.append(den.transpose(0, 1, 3, 2).reshape(b, h, Q_BLOCK))
            maxs.append(m[..., 0].transpose(0, 1, 3, 2).reshape(b, h, Q_BLOCK))
        num = jnp.stack(nums)
        den = jnp.stack(dens)
        mx = jnp.stack(maxs)
        wgt = jnp.exp(mx - jnp.max(mx, axis=0, keepdims=True))
        out = jnp.sum(num * wgt[..., None], axis=0) / jnp.sum(den * wgt, axis=0)[..., None]
        return out.astype(q.dtype)

    out = lax.map(block, (qb, jnp.arange(n_blocks)))
    return out.transpose(1, 2, 0, 3, 4).reshape(b, h, s, dh)

def forgetting_attention(q, k, v, log_f):
    b, h, s, dh = q.shape
    n_blocks = s // Q_BLOCK
    c = jnp.cumsum(log_f, axis=-1)
    qb = q.reshape(b, h, n_blocks, Q_BLOCK, dh).transpose(2, 0, 1, 3, 4)
    cb = c.reshape(b, h, n_blocks, Q_BLOCK).transpose(2, 0, 1, 3)
    kpos = jnp.arange(s)

    def block(args):
        qblk, cq, blk = args
        sc = jnp.einsum('bhqd,bhkd->bhqk', qblk, k, preferred_element_type=jnp.float32)
        sc = sc + cq[..., :, None] - c[:, :, None, :]
        qpos = blk * Q_BLOCK + jnp.arange(Q_BLOCK)
        sc = jnp.where(kpos[None, :] <= qpos[:, None], sc, -jnp.inf)
        p = jax.nn.softmax(sc, axis=-1)
        return jnp.einsum('bhqk,bhkd->bhqd', p.astype(v.dtype), v)

    out = lax.map(block, (qb, cb, jnp.arange(n_blocks)))
    return out.transpose(1, 2, 0, 3, 4).reshape(b, h, s, dh)

def setup_inputs(seed: int = 0) -> dict:
    key = jax.random.key(seed)
    ks = jax.random.split(key, 20)
    f32 = jnp.float32

    def w(k, shape, fan_in):
        return jax.random.normal(k, shape, f32) * fan_in ** -0.5

    def gain(k):
        return 1.0 + 0.02 * jax.random.normal(k, (DEPTH, D_MODEL), f32)

    return {
        "x": jax.random.normal(ks[0], (BATCH, SEQ, D_MODEL), f32),
        "ffn1_norm": gain(ks[1]),
        "ffn1_w_gate": w(ks[2], (DEPTH, D_MODEL, D_FF), D_MODEL),
        "ffn1_w_up": w(ks[3], (DEPTH, D_MODEL, D_FF), D_MODEL),
        "ffn1_w_down": w(ks[4], (DEPTH, D_FF, D_MODEL), D_FF),
        "mix_norm": gain(ks[5]),
        "w_in": w(ks[6], (DEPTH, D_MODEL, IN_COLS), D_MODEL),
        "b_forget": 4.0 + jax.random.normal(ks[7], (DEPTH, N_HEADS_FOX), f32),
        "b_gate_dil": 0.02 * jax.random.normal(ks[8], (DEPTH, D_MODEL), f32),
        "b_gate_fox": 0.02 * jax.random.normal(ks[9], (DEPTH, D_MODEL), f32),
        "w_proj_dil": w(ks[10], (DEPTH, D_DIL, D_MODEL), D_DIL),
        "w_proj_fox": w(ks[11], (DEPTH, D_FOX, D_MODEL), D_FOX),
        "w_out": w(ks[12], (DEPTH, D_MODEL, D_MODEL), D_MODEL),
        "ffn2_norm": gain(ks[13]),
        "ffn2_w_gate": w(ks[14], (DEPTH, D_MODEL, D_FF), D_MODEL),
        "ffn2_w_up": w(ks[15], (DEPTH, D_MODEL, D_FF), D_MODEL),
        "ffn2_w_down": w(ks[16], (DEPTH, D_FF, D_MODEL), D_FF),
        "final_norm": 1.0 + 0.02 * jax.random.normal(ks[17], (D_MODEL,), f32),
    }

def reference(x, ffn1_norm, ffn1_w_gate, ffn1_w_up, ffn1_w_down, mix_norm, w_in,
              b_forget, b_gate_dil, b_gate_fox, w_proj_dil, w_proj_fox, w_out,
              ffn2_norm, ffn2_w_gate, ffn2_w_up, ffn2_w_down, final_norm):
    split_points = list(np.cumsum(IN_SPLITS)[:-1])
    scale = HEAD_DIM ** -0.5
    for l in range(DEPTH):
        x = x + 0.5 * swiglu(rmsnorm(x, ffn1_norm[l]), ffn1_w_gate[l], ffn1_w_up[l], ffn1_w_down[l])

        h = rmsnorm(x, mix_norm[l])
        proj = h @ w_in[l]
        q_d, k_d, v_d, q_f, k_f, v_f, f_logit, g_d, g_f = jnp.split(proj, split_points, axis=-1)

        qa = partial_rope(split_heads(q_d, N_HEADS_DIL)) * scale
        ka = partial_rope(split_heads(k_d, N_HEADS_DIL))
        va = split_heads(v_d, N_HEADS_DIL)
        y_dil = merge_heads(dilated_attention(qa, ka, va))

        log_f = jax.nn.log_sigmoid((f_logit + b_forget[l]).astype(jnp.float32))
        log_f = log_f.transpose(0, 2, 1)
        qb_ = split_heads(q_f, N_HEADS_FOX) * scale
        kb_ = split_heads(k_f, N_HEADS_FOX)
        vb_ = split_heads(v_f, N_HEADS_FOX)
        y_fox = merge_heads(forgetting_attention(qb_, kb_, vb_, log_f))

        merged = (jax.nn.sigmoid(g_d + b_gate_dil[l]) * (y_dil @ w_proj_dil[l])
                  + jax.nn.sigmoid(g_f + b_gate_fox[l]) * (y_fox @ w_proj_fox[l]))
        x = x + merged @ w_out[l]

        x = x + 0.5 * swiglu(rmsnorm(x, ffn2_norm[l]), ffn2_w_gate[l], ffn2_w_up[l], ffn2_w_down[l])
    return rmsnorm(x, final_norm)


_drawn_inputs = setup_inputs


def setup_inputs(seed=0):
    import zlib

    import numpy as np

    out = dict(_drawn_inputs(seed))
    spreads = {}
    factors = {'ffn1_norm': 6.193,
     'mix_norm': 8.0,
     'b_gate_dil': 49.476,
     'b_gate_fox': 47.422,
     'ffn2_norm': 7.144,
     'final_norm': 7.996}
    for name, (base, spread) in spreads.items():
        noise = np.random.default_rng([zlib.crc32(name.encode()), seed]).standard_normal(out[name].shape)
        drawn = base * np.exp(spread * noise) if base else spread * noise
        out[name] = __import__('jax').numpy.asarray(drawn.astype(out[name].dtype))
    for name, factor in factors.items():
        out[name] = (out[name] * factor).astype(out[name].dtype)
    return out
```

```python
import numpy as np

import concourse.bass as bass
from concourse import mybir

F32 = mybir.dt.float32
F32R = mybir.dt.float32r
BF16 = mybir.dt.bfloat16
ALU = mybir.AluOpType
ACT = mybir.ActivationFunctionType
AXIS_X = mybir.AxisListType.X

P = 128
SEQ = 256
TT = SEQ // P
D_MODEL = 2048
D_FF = 5632
HEADS = 8
D_MIX = HEADS * P
ROPE_DIM = P // 4
HALF = ROPE_DIM // 2
ROPE_THETA = 500000.0
PATTERNS = ((128, 1), (512, 4), (2048, 16))
EPS = 1e-6
SCALE = float(P) ** -0.5
MASKED = -1e30

CH = 512
KT = D_MODEL // P
CT = CH // P
NN = D_MODEL // CH
FF_CHUNKS = D_FF // CH
F_COL = 6 * D_MIX
G_COL = F_COL + HEADS

SLOTS = 4
LOADS = 4
AHEAD = SLOTS

WIDE, HALF_W, DOWN = 8, 4, 8
FFN_STEP = 2 * WIDE + DOWN
FFN_SLABS = FF_CHUNKS * FFN_STEP
MIX = FFN_SLABS
QKV_STEP = 3 * WIDE
FOX = MIX + 2 * QKV_STEP
MERGE = FOX + 2 * QKV_STEP
MERGE_FIRST = 2 * WIDE + 2 * HALF_W
MERGE_STEP = MERGE_FIRST + DOWN
MERGE_LAST = MERGE + MERGE_FIRST + (NN - 1) * MERGE_STEP
FFN2 = MERGE_LAST + DOWN
TOTAL = FFN2 + FFN_SLABS

C_ID, C_CUM, C_DIL, C_COS, C_SIN, C_TRI, C_END = 0, 128, 384, 640, 704, 768, 896


def constants():
    c = np.zeros((P, C_END), np.float32)
    p = np.arange(P)
    c[:, C_ID:C_ID + P] = np.eye(P)
    c[:, C_CUM:C_CUM + P] = p[:, None] <= p[None, :]
    c[:, C_CUM + P:C_CUM + 2 * P] = 1.0
    gap = P + p[:, None] - np.arange(2 * P)[None, :]
    seen = sum(((gap >= 0) & (gap <= w) & (gap % d == 0)).astype(int) for w, d in PATTERNS)
    c[:, C_DIL:C_DIL + 2 * P] = np.where(seen > 0, np.log(np.maximum(seen, 1)), MASKED)
    inv_freq = np.float32(ROPE_THETA) ** (-np.arange(0, ROPE_DIM, 2, dtype=np.float32) / ROPE_DIM)
    for t in range(TT):
        ang = (t * P + p).astype(np.float32)[:, None] * inv_freq[None, :].astype(np.float32)
        at = t * ROPE_DIM
        c[:, C_COS + at:C_COS + at + ROPE_DIM] = np.tile(np.cos(ang), 2)
        c[:, C_SIN + at:C_SIN + at + ROPE_DIM] = np.concatenate([np.sin(ang), -np.sin(ang)], 1)
    c[:, C_TRI:C_TRI + P] = np.where(p[None, :] <= p[:, None], 0.0, MASKED)
    return c


class Place:

    def __init__(self, start, per=0, i=None):
        assert start % 8 == 0 and per % 8 == 0
        self.start, self.per, self.i = start, per, i

    def slab(self, offset):
        n = self.start + offset
        return n if self.i is None else self.i * self.per + n

    def turn(self, offset):
        n = (self.start + offset) // 8
        return n if self.i is None else self.i * (self.per // 8) + n


def build(nc, x, ffn1_norm, ffn1_w_gate, ffn1_w_up, ffn1_w_down, mix_norm, w_in, b_forget,
          b_gate_dil, b_gate_fox, w_proj_dil, w_proj_fox, w_out, ffn2_norm, ffn2_w_gate,
          ffn2_w_up, ffn2_w_down, final_norm, out):
    table = nc.inline_tensor(constants(), name="shape_tables").ap()

    def rows(w):
        return w.rearrange("l (a p) n -> (l p) a n", p=P)

    gate_w = (rows(ffn1_w_gate), rows(ffn2_w_gate))
    up_w = (rows(ffn1_w_up), rows(ffn2_w_up))
    down_w = (rows(ffn1_w_down), rows(ffn2_w_down))
    in_w, out_w = rows(w_in), rows(w_out)
    proj_w = (rows(w_proj_dil), rows(w_proj_fox))
    x_rows = x.rearrange("b (t p) n -> (b p) t n", p=P)
    out_rows = out.rearrange("b (t p) n -> (b p) t n", p=P)

    def sb(name, shape, dt=F32):
        return nc.alloc_sbuf_tensor(name, shape, dt)

    xres = sb("xres", [P, TT, D_MODEL])
    xT_hi = sb("xT_hi", [P, KT, SEQ], F32R)
    xT_lo = sb("xT_lo", [P, KT, SEQ], F32R)
    raw = sb("raw", [P, LOADS, CT, CH])
    w_hi = sb("w_hi", [P, SLOTS, 2, CH], F32R)
    w_lo = sb("w_lo", [P, SLOTS, 2, CH], F32R)
    hT_hi = sb("hT_hi", [P, CT, SEQ], F32R)
    hT_lo = sb("hT_lo", [P, CT, SEQ], F32R)
    qT_at = nc.sbuf_base
    qT = sb("qT", [P, 2 * HEADS, SEQ])
    kT_at = nc.sbuf_base
    kT = sb("kT", [P, 2 * HEADS, SEQ])
    assert kT_at - qT_at == nc.sbuf_base - kT_at == 2 * HEADS * SEQ * 4
    yT_hi = nc.alloc_sbuf_tensor_at("yT_hi", [P, 2 * HEADS, SEQ], F32R, offset=qT_at)
    yT_lo = nc.alloc_sbuf_tensor_at("yT_lo", [P, 2 * HEADS, SEQ], F32R, offset=kT_at)
    final_gain = nc.alloc_sbuf_tensor_at("final_gain", [P, D_MODEL], F32, offset=qT_at)
    v_sb = sb("v_sb", [P, TT, 2 * D_MIX])
    chunk_buf = sb("chunk_buf", [P, TT, CH])
    hidden = sb("hidden", [P, TT, CH])
    gate_buf = sb("gate_buf", [P, 2, TT, CH])
    gate_bias = sb("gate_bias", [P, 2, CH])
    probs = sb("probs", [P, 3 * P])
    probsT = sb("probsT", [P, 3 * P])
    tab = sb("tab", [P, C_END])
    ident_b = sb("ident_b", [P, P], BF16)
    tri_b = sb("tri_b", [P, P], BF16)
    rope_a = sb("rope_a", [P, TT, CT, ROPE_DIM])
    rope_b = sb("rope_b", [P, TT, CT, ROPE_DIM])
    f_raw = sb("f_raw", [P, KT, HEADS])
    f_hi = sb("f_hi", [P, KT, HEADS], F32R)
    f_lo = sb("f_lo", [P, KT, HEADS], F32R)
    f_bias = sb("f_bias", [P, HEADS])
    f_z = sb("f_z", [P, TT, HEADS])
    f_abs = sb("f_abs", [P, TT, HEADS])
    f_soft = sb("f_soft", [P, TT, HEADS])
    f_neg = sb("f_neg", [P, TT, HEADS])
    gain_rows = sb("gain_rows", [3 * KT, P])
    gains = sb("gains", [P, 3 * KT])
    squares = sb("squares", [P, TT, NN])
    mean = sb("mean", [P, TT])
    root = sb("root", [P, TT])
    rstd = sb("rstd", [P, TT])
    rstd_q = sb("rstd_q", [P, TT])
    newton = sb("newton", [P, TT])
    neg_max = sb("neg_max", [P, TT])
    denom = sb("denom", [P, TT])
    inv_denom = sb("inv_denom", [P, TT])

    ps = nc.alloc_psum_tensor("ps", [P, 8, CH], F32)
    A, B, C, T = 0, 2, 4, 6
    SCORES, PROBS_T, QK_T, HEAD_OUT = 4, 5, 6, 7


    ident = tab[:, C_ID:C_ID + P]
    cum = tab[:, C_CUM:C_CUM + 2 * P]
    dil_bias = tab[:, C_DIL:C_DIL + 2 * P]

    def sem(name):
        return nc.alloc_semaphore(name)

    raw_landed = [sem(f"raw_landed{n}") for n in range(LOADS)]
    x_landed = [sem(f"x_landed{n}") for n in range(NN)]
    table_landed = sem("table_landed")
    gains_landed = sem("gains_landed")
    forget_landed = sem("forget_landed")
    gate_bias_landed = sem("gate_bias_landed")
    final_gain_landed = sem("final_gain_landed")
    stored = sem("stored")
    hi_ready = sem("hi_ready")
    lo_ready = sem("lo_ready")
    slab_done = sem("slab_done")
    gains_raw = sem("gains_raw")
    gains_ready = sem("gains_ready")
    consts_ready = sem("consts_ready")
    xt_raw = sem("xt_raw")
    xt_scaled = sem("xt_scaled")
    xt_hi = sem("xt_hi")
    xt_lo = sem("xt_lo")
    squared = sem("squared")
    mean_ready = sem("mean_ready")
    root_ready = sem("root_ready")
    rstd_ready = sem("rstd_ready")
    small = sem("small")
    silu_done = sem("silu_done")
    hidden_ready = sem("hidden_ready")
    ht_raw = sem("ht_raw")
    ht_hi = sem("ht_hi")
    ht_lo = sem("ht_lo")
    added = sem("added")
    evac = sem("evac")
    rotated = sem("rotated")
    turned = sem("turned")
    qk_raw = sem("qk_raw")
    qk_out = sem("qk_out")
    f_split = sem("f_split")
    f_split_lo = sem("f_split_lo")
    f_done = sem("f_done")
    f_z_ready = sem("f_z_ready")
    f_abs_ready = sem("f_abs_ready")
    f_exp = sem("f_exp")
    f_soft_ready = sem("f_soft_ready")
    f_ready = sem("f_ready")
    scores = sem("scores")
    rowmax = sem("rowmax")
    exped = sem("exped")
    normed = sem("normed")
    pt_raw = sem("pt_raw")
    pt_copied = sem("pt_copied")
    head_out = sem("head_out")
    y_hi = sem("y_hi")
    y_lo = sem("y_lo")
    gate_pre = sem("gate_pre")
    gate_done = sem("gate_done")
    gated = sem("gated")
    out_ready = sem("out_ready")

    ADDED = {0: 0, "mix": FF_CHUNKS * NN * TT, 1: (FF_CHUNKS + NN) * NN * TT}
    HID = {0: 0, "mix": FF_CHUNKS * TT, 1: (FF_CHUNKS + NN) * TT}

    QK_TILES = 2 * 2 * TT
    QKV_TILES = 3 * 2 * TT

    DIL_SLOTS = {4 + 4 * s: s for s in range(HEADS + 2)}
    FOX_SLOTS = {2 * s: s for s in range(HEADS + 2)}

    block = nc.Block()
    with block:

        @block.sync
        def _(sp):
            for n in range(NN):
                sp.dma_start(xres[:, :, n * CH:(n + 1) * CH],
                             x_rows[:, :, n * CH:(n + 1) * CH]).then_inc(x_landed[n], 16)

            def load(place, offset, src):
                u = (place.start + offset) // 2
                if place.start + offset >= 2 * LOADS:
                    sp.wait_ge(lo_ready, place.slab(offset - 2 * LOADS + 2))
                sp.dma_start(raw[:, u % LOADS], src).then_inc(raw_landed[u % LOADS], 16)

            def load_wide(place, offset, w, cols, k_tiles=KT):
                for kk in range(k_tiles // CT):
                    load(place, offset + 2 * kk, w[:, CT * kk:CT * (kk + 1), cols])

            def load_down(place, offset, w, k_tile):
                for n in range(NN):
                    load(place, offset + 2 * n, w[:, k_tile, n * CH:(n + 1) * CH])

            def ffn(f, start):
                first = Place(start)
                load_wide(first, 0, gate_w[f], slice(0, CH))
                load_wide(first, WIDE, up_w[f], slice(0, CH))
                with sp.Fori(0, FF_CHUNKS - 1) as i:
                    place = Place(start + 2 * WIDE, FFN_STEP, i)
                    load_wide(place, 0, gate_w[f], bass.ds(i * CH + CH, CH))
                    load_wide(place, WIDE, up_w[f], bass.ds(i * CH + CH, CH))
                    load_down(place, 2 * WIDE, down_w[f], bass.ds(i * CT, CT))
                load_down(Place(start + FFN_SLABS - DOWN), 0, down_w[f],
                          slice((FF_CHUNKS - 1) * CT, FF_CHUNKS * CT))

            ffn(0, 0)
            with sp.Fori(0, 2) as i:
                place = Place(MIX, QKV_STEP, i)
                for part in range(3):
                    load_wide(place, part * WIDE, in_w, bass.ds(i * CH + part * D_MIX, CH))
            with sp.Fori(0, 2) as i:
                place = Place(FOX, QKV_STEP, i)
                for part in range(3):
                    load_wide(place, part * WIDE, in_w, bass.ds(i * CH + (3 + part) * D_MIX, CH))

            def merge(place, n, cols, proj_cols, gd_cols, gf_cols):
                if not (n is None):
                    sp.wait_ge(gate_pre, n * (2 * TT))
                for g, b in enumerate((b_gate_dil, b_gate_fox)):
                    sp.dma_start(gate_bias[:, g, :], b[:, cols].broadcast_to([P, CH]))\
                      .then_inc(gate_bias_landed, 16)
                load_wide(place, 0, in_w, gd_cols)
                load_wide(place, WIDE, in_w, gf_cols)
                load_wide(place, 2 * WIDE, proj_w[0], proj_cols, HEADS)
                load_wide(place, 2 * WIDE + HALF_W, proj_w[1], proj_cols, HEADS)

            merge(Place(MERGE), None, slice(0, CH), slice(0, CH), slice(G_COL, G_COL + CH),
                  slice(G_COL + D_MODEL, G_COL + D_MODEL + CH))
            with sp.Fori(0, NN - 1) as i:
                place = Place(MERGE + MERGE_FIRST, MERGE_STEP, i)
                cols = bass.ds(i * CH + CH, CH)
                merge(place, i + 1, cols, cols, bass.ds(i * CH + (G_COL + CH), CH),
                      bass.ds(i * CH + (G_COL + D_MODEL + CH), CH))
                load_down(place, MERGE_FIRST, out_w, bass.ds(i * CT, CT))
            load_down(Place(MERGE_LAST), 0, out_w, slice((NN - 1) * CT, NN * CT))
            sp.wait_ge(slab_done, MERGE_LAST - DOWN)
            sp.dma_start(final_gain[:, :], final_norm.rearrange("(a n) -> a n", a=1)
                         .broadcast_to([P, D_MODEL])).then_inc(final_gain_landed, 16)
            ffn(1, FFN2)
            for n in range(NN):
                sp.wait_ge(out_ready, TT * (n + 1))
                sp.dma_start(out_rows[:, :, n * CH:(n + 1) * CH],
                             xres[:, :, n * CH:(n + 1) * CH]).then_inc(stored, 16)
            sp.wait_ge(stored, 16 * NN)

        def tokens(t):
            return slice(t * P, (t + 1) * P)

        def chunk(n):
            return slice(n * CH, (n + 1) * CH)

        def down_banks(n):
            return A if n % 2 == 0 else C

        def tiles(ap):
            return ap.rearrange("p (k c) -> p k c", c=P)

        @block.tensor
        def _(pe):
            def slab(place, offset, banks, lhs, k0, first, last):
                s = (place.start + offset) % SLOTS
                pe.wait_ge(lo_ready, place.slab(offset + 1))
                for j in range(2):
                    for t in range(TT):
                        hi, lo = lhs(k0 + j, t)
                        acc = ps[:, banks + t, :]
                        nc.tensor.matmul(acc, hi, w_hi[:, s, j], start=first and j == 0, stop=False)
                        nc.tensor.matmul(acc, hi, w_lo[:, s, j], start=False, stop=False)
                        done = nc.tensor.matmul(acc, lo, w_hi[:, s, j], start=False,
                                                stop=last and j == 1)
                done.then_inc(slab_done, 1)

            def of_x(k, t):
                return xT_hi[:, k, tokens(t)], xT_lo[:, k, tokens(t)]

            def of_hidden(k, t):
                return hT_hi[:, k, tokens(t)], hT_lo[:, k, tokens(t)]

            def wide(place, offset, banks, o):
                slab(place, offset + o, banks, of_x, 2 * o, o == 0, o == WIDE - 1)

            def wide_all(place, offset, banks):
                for o in range(WIDE):
                    wide(place, offset, banks, o)

            def transpose_x(b, n):
                for t in range(TT):
                    if b == 0:
                        pe.wait_ge(x_landed[n], 16)
                    else:
                        pe.wait_ge(added, (0, ADDED["mix"], ADDED[1])[b] - (NN - n) * TT + t + 1)
                    if n > 0:
                        pe.wait_ge(xt_scaled, (b * NN + n - 1) * TT + t + 1)
                    for k in range(CT):
                        done = nc.tensor.transpose(ps[:, T + t, k * P:(k + 1) * P],
                                                   xres[:, t, n * CH + k * P:n * CH + (k + 1) * P], ident)
                    done.then_inc(xt_raw, 1)

            def wide_at_boundary(place, b, banks):
                for o in range(WIDE):
                    if o % 2 == 0:
                        pe.wait_ge(xt_lo, (b * NN + o // 2 + 1) * TT)
                    wide(place, 0, banks, o)
                    if o == 1:
                        transpose_x(b, NN - 1)

            def transpose_hidden(count):
                for t in range(TT):
                    pe.wait_ge(hidden_ready, count + t + 1)
                    for k in range(CT):
                        done = nc.tensor.transpose(ps[:, T + t, k * P:(k + 1) * P],
                                                   hidden[:, t, k * P:(k + 1) * P], ident)
                    done.then_inc(ht_raw, 1)

            def down(place, offset, count, base, boundary=None):
                pe.wait_ge(ht_lo, count + TT)
                for n in range(NN):
                    if n >= 2:
                        pe.wait_ge(added, base + (n - 1) * TT)
                    for o in range(2):
                        slab(place, offset + 2 * n + o, down_banks(n), of_hidden, 2 * o, o == 0, o == 1)
                    if boundary is not None and n > 0:
                        transpose_x(boundary, n - 1)

            def ffn(f, start, b):
                hid, base = HID[f], ADDED[f]
                silu = f * FF_CHUNKS * TT
                first = Place(start)
                wide_at_boundary(first, b, A)
                wide_all(first, WIDE, B)
                with pe.Fori(0, FF_CHUNKS - 1) as i:
                    place = Place(start + 2 * WIDE, FFN_STEP, i)
                    pe.wait_ge(silu_done, i * TT + (silu + TT))
                    wide_all(place, 0, A)
                    transpose_hidden(i * TT + hid)
                    wide_all(place, WIDE, B)
                    pe.wait_ge(silu_done, i * TT + (silu + 2 * TT))
                    down(place, 2 * WIDE, i * TT + hid, i * (NN * TT) + base)
                    pe.wait_ge(added, i * (NN * TT) + (base + (NN - 1) * TT))
                transpose_hidden(hid + (FF_CHUNKS - 1) * TT)
                down(Place(start + FFN_SLABS - DOWN), 0, hid + (FF_CHUNKS - 1) * TT,
                     base + (FF_CHUNKS - 1) * NN * TT, 1 if f == 0 else None)

            def transpose_qk(t, count, from_sem, from_count):
                pe.wait_ge(from_sem, from_count)
                if t > 0:
                    pe.wait_ge(qk_out, count)
                for k in range(CT):
                    done = nc.tensor.transpose(ps[:, QK_T, k * P:(k + 1) * P],
                                               chunk_buf[:, t, k * P:(k + 1) * P], ident)
                done.then_inc(qk_raw, 1)

            def head_scores(h):
                q, k = qT[:, h, :], kT[:, h, :]
                if h == 0:
                    pe.wait_ge(f_z_ready, TT)
                    pe.wait_ge(qk_out, QK_TILES)
                if h == HEADS:
                    pe.wait_ge(qk_out, 2 * QK_TILES)
                    pe.wait_ge(f_ready, 1)
                if h > 0:
                    pe.wait_ge(exped, h * TT)
                early, late = ps[:, SCORES, 0:P], ps[:, SCORES, P:3 * P]
                if h < HEADS:
                    nc.tensor.matmul(early, q[:, 0:P], k[:, 0:P], start=True, stop=False)
                    nc.tensor.matmul(early, ident, dil_bias[:, P:2 * P], start=False, stop=True)
                    nc.tensor.matmul(late, q[:, P:2 * P], k, start=True, stop=False)
                    done = nc.tensor.matmul(late, ident, dil_bias, start=False, stop=True)
                else:
                    neg = [f_neg[:, t, h - HEADS:h - HEADS + 1].broadcast_to([P, P]) for t in range(TT)]
                    diag = ps[:, SCORES, 2 * P:3 * P]
                    nc.tensor.matmul(early, q[:, 0:P], k[:, 0:P], start=True, stop=False)
                    nc.tensor.matmul(early, neg[0], cum[:, 0:P], start=False, stop=False)
                    nc.tensor.matmul(early, ident_b[:, :], tri_b[:, :], start=False, stop=True)
                    nc.tensor.matmul(late, q[:, P:2 * P], k, start=True, stop=False)
                    nc.tensor.matmul(late, neg[0], cum, start=False, stop=False)
                    nc.tensor.matmul(diag, neg[1], cum[:, 0:P], start=False, stop=False)
                    done = nc.tensor.matmul(diag, ident_b[:, :], tri_b[:, :], start=False, stop=True)
                done.then_inc(scores, 1)

            def head_transpose(h):
                pe.wait_ge(normed, (h + 1) * TT)
                if h > 0:
                    pe.wait_ge(pt_copied, h)
                for part in range(3):
                    done = nc.tensor.transpose(ps[:, PROBS_T, part * P:(part + 1) * P],
                                               probs[:, part * P:(part + 1) * P], ident)
                done.then_inc(pt_raw, 1)

            def head_values(h):
                pe.wait_ge(pt_copied, h + 1)
                if h % HEADS == 0:
                    pe.wait_ge(evac, (h // HEADS + 1) * QKV_TILES)
                if h > 0:
                    pe.wait_ge(y_lo, h)
                nc.tensor.matmul(ps[:, HEAD_OUT, 0:2 * P], v_sb[:, 0, h * P:(h + 1) * P],
                                 probsT[:, 0:2 * P], start=True, stop=False)
                nc.tensor.matmul(ps[:, HEAD_OUT, P:2 * P], v_sb[:, 1, h * P:(h + 1) * P],
                                 probsT[:, 2 * P:3 * P], start=False, stop=True).then_inc(head_out, 1)

            def attend(s, h0):
                if s >= 2:
                    head_values(h0 + s - 2)
                if 1 <= s <= HEADS:
                    head_transpose(h0 + s - 1)
                if s < HEADS:
                    head_scores(h0 + s)

            pe.wait_ge(table_landed, 16)
            pe.wait_ge(gains_landed, 48)
            nc.tensor.transpose(ps[:, T, 0:3 * KT], gain_rows[:, :], ident[0:3 * KT, 0:3 * KT])\
              .then_inc(gains_raw, 1)
            pe.wait_ge(gains_ready, 1)
            for n in range(NN - 1):
                transpose_x(0, n)
            ffn(0, 0, 0)

            transpose_x(1, NN - 1)
            with pe.Fori(0, 2) as i:
                place = Place(MIX, QKV_STEP, i)
                for part, banks in enumerate((A, B, C)):
                    for o in range(WIDE):
                        if part == 0 and o % 2 == 0:
                            pe.wait_ge(xt_lo, (NN + o // 2 + 1) * TT)
                        wide(place, part * WIDE, banks, o)
                        if part > 0 and o in (2, 4):
                            t = o // 2 - 1
                            transpose_qk(t, i * (2 * TT) + ((part - 1) * TT + t), rotated, i * 4 + 2 * part)

            place = Place(FOX)
            for c in range(6):
                half, part = divmod(c, 3)
                banks = A if c % 2 == 0 else B
                pe.wait_ge(evac, QKV_TILES + (c - 1) * TT)
                for o in range(WIDE):
                    e = c * WIDE + o
                    wide(place, c * WIDE, banks, o)
                    if e == 1:
                        pe.wait_ge(evac, QKV_TILES)
                        pe.wait_ge(f_split_lo, 1)
                        for t in range(TT):
                            for k in range(KT):
                                hi, lo = of_x(k, t)
                                acc = ps[:, C + t, 0:HEADS]
                                nc.tensor.matmul(acc, hi, f_hi[:, k], start=k == 0, stop=False)
                                nc.tensor.matmul(acc, hi, f_lo[:, k], start=False, stop=False)
                                done = nc.tensor.matmul(acc, lo, f_hi[:, k], start=False, stop=k == KT - 1)
                            done.then_inc(f_done, 1)
                    if part > 0 and o in (2, 4):
                        t = o // 2 - 1
                        transpose_qk(t, QK_TILES + (half * 2 + part - 1) * TT + t, evac,
                                     QKV_TILES + c * TT)
                    if e in DIL_SLOTS:
                        attend(DIL_SLOTS[e], 0)

            def project(place, offset, g, banks):
                def of_y(k, t):
                    return yT_hi[:, g * HEADS + k, tokens(t)], yT_lo[:, g * HEADS + k, tokens(t)]

                for o in range(HALF_W):
                    slab(place, offset + o, banks, of_y, 2 * o, o == 0, o == HALF_W - 1)
                    yield o

            place = Place(MERGE)
            e = 0
            for g, banks in enumerate((A, B)):
                pe.wait_ge(evac, 2 * QKV_TILES - (1 - g) * TT)
                for o in range(WIDE):
                    wide(place, g * WIDE, banks, o)
                    if e in FOX_SLOTS:
                        attend(FOX_SLOTS[e], HEADS)
                    e += 1
            for g, banks in enumerate((A, B)):
                pe.wait_ge(gate_pre, (g + 1) * TT)
                pe.wait_ge(y_lo, (g + 1) * HEADS)
                for _ in project(place, 2 * WIDE + g * HALF_W, g, banks):
                    if e in FOX_SLOTS:
                        attend(FOX_SLOTS[e], HEADS)
                    e += 1

            with pe.Fori(0, NN - 1) as i:
                place = Place(MERGE + MERGE_FIRST, MERGE_STEP, i)
                for g, banks in enumerate((A, B)):
                    pe.wait_ge(gated, i * (2 * TT) + (g + 1) * TT)
                    wide_all(place, g * WIDE, banks)
                    if g == 0:
                        transpose_hidden(i * TT + HID["mix"])
                for g, banks in enumerate((A, B)):
                    pe.wait_ge(gate_pre, i * (2 * TT) + (2 + g + 1) * TT)
                    for _ in project(place, 2 * WIDE + g * HALF_W, g, banks):
                        pass
                pe.wait_ge(gated, i * (2 * TT) + (2 + 1) * TT)
                down(place, MERGE_FIRST, i * TT + HID["mix"], i * (NN * TT) + ADDED["mix"])
                pe.wait_ge(added, i * (NN * TT) + (ADDED["mix"] + (NN - 1) * TT))
            transpose_hidden(HID["mix"] + (NN - 1) * TT)
            down(Place(MERGE_LAST), 0, HID["mix"] + (NN - 1) * TT,
                 ADDED["mix"] + (NN - 1) * NN * TT, 2)
            ffn(1, FFN2, 2)

        @block.scalar
        def _(act):
            act.dma_start(tab[:, :], table).then_inc(table_landed, 16)
            for n, g in enumerate((ffn1_norm, mix_norm, ffn2_norm)):
                act.dma_start(gain_rows[n * KT:(n + 1) * KT, :],
                              g.rearrange("l (k p) -> (l k) p", p=P)).then_inc(gains_landed, 16)
            act.dma_start(f_raw[:, :, :], in_w[:, :, F_COL:G_COL]).then_inc(forget_landed, 16)
            act.dma_start(f_bias[:, :], b_forget.broadcast_to([P, HEADS])).then_inc(forget_landed, 16)

            def round_slab(place, offset):
                n = place.start + offset
                if n >= TOTAL:
                    return
                if n % 2 == 0:
                    act.wait_ge(raw_landed[n // 2 % LOADS], place.turn(offset) * 16 + 16)
                if n >= SLOTS:
                    act.wait_ge(slab_done, place.slab(offset - SLOTS + 1))
                nc.scalar.activation(w_hi[:, n % SLOTS], raw[:, n // 2 % LOADS, n % 2 * 2:n % 2 * 2 + 2, :],
                                     ACT.Copy).then_inc(hi_ready, 1)

            def round_x(b, n):
                for t in range(TT):
                    count = (b * NN + n) * TT + t + 1
                    act.wait_ge(xt_scaled, count)
                    nc.scalar.activation(xT_hi[:, n * CT:(n + 1) * CT, tokens(t)], tiles(hidden[:, t]),
                                         ACT.Copy).then_inc(xt_hi, 1)

            def square(b, n):
                for t in range(TT):
                    if b == 0:
                        act.wait_ge(x_landed[n], 16)
                    else:
                        act.wait_ge(added, (0, ADDED["mix"], ADDED[1], ADDED[1] + ADDED["mix"])[b]
                                    - (NN - n) * TT + t + 1)
                    if n > 0:
                        act.wait_ge(squared, (b * NN + n - 1) * TT + t + 1)
                    nc.scalar.activation(chunk_buf[:, t], xres[:, t, chunk(n)], ACT.Square,
                                         accum_out=squares[:, t, n:n + 1]).then_inc(squared, 1)

            def take_root(b):
                act.wait_ge(mean_ready, b + 1)
                nc.scalar.activation(root[:, :], mean[:, :], ACT.Sqrt).then_inc(root_ready, 1)

            def round_hidden(count):
                for t in range(TT):
                    act.wait_ge(ht_raw, count + t + 1)
                    nc.scalar.activation(hT_hi[:, :, tokens(t)], tiles(ps[:, T + t]), ACT.Copy)\
                      .then_inc(ht_hi, 1)

            def silu(place, offset, b, used):
                act.wait_ge(rstd_ready, b + 1)
                act.wait_ge(slab_done, place.slab(offset))
                if used is not None:
                    act.wait_ge(hidden_ready, used)
                for t in range(TT):
                    nc.scalar.activation(chunk_buf[:, t], ps[:, A + t], ACT.Silu,
                                         scale=rstd[:, t:t + 1]).then_inc(silu_done, 1)

            def last_down(start, b):
                place = Place(start)
                for o in range(DOWN):
                    round_slab(place, o + AHEAD)
                    if o % 2 == 1:
                        square(b, o // 2)
                        if b < 3 and o > 1:
                            round_x(b, o // 2 - 1)

            def ffn(f, start, b):
                first = Place(start)
                for o in range(2 * WIDE):
                    round_slab(first, o + AHEAD)
                    if o == 1:
                        round_x(b, NN - 1)
                    if b == 0 and o < NN:
                        square(0, o)
                    if o == NN:
                        take_root(b)
                    if o == WIDE - 1:
                        silu(first, WIDE, b, None)
                with act.Fori(0, FF_CHUNKS - 1) as i:
                    place = Place(start + 2 * WIDE, FFN_STEP, i)
                    for o in range(FFN_STEP):
                        round_slab(place, o + AHEAD)
                        if o == WIDE - 1:
                            silu(place, WIDE, b, i * TT + (HID[f] + TT))
                            round_hidden(i * TT + HID[f])
                round_hidden(HID[f] + (FF_CHUNKS - 1) * TT)
                last_down(start + FFN_SLABS - DOWN, b + 1)

            for n in range(NN - 1):
                round_x(0, n)
            for o in range(AHEAD):
                round_slab(Place(0), o)
            ffn(0, 0, 0)
            round_x(1, NN - 1)
            take_root(1)

            def evacuate(place, offset, part, banks, v_cols):
                act.wait_ge(rstd_ready, 2)
                act.wait_ge(slab_done, place.slab(offset))
                for t in range(TT):
                    dst = chunk_buf[:, t] if part < 2 else v_sb[:, t, v_cols]
                    factor = (rstd_q if part == 0 else rstd)[:, t:t + 1]
                    nc.scalar.activation(dst, ps[:, banks + t], ACT.Copy, scale=factor)\
                      .then_inc(evac, 1)

            def copy_qk(part, heads, t, count):
                act.wait_ge(qk_raw, count + 1)
                nc.scalar.activation((qT, kT)[part][:, heads, tokens(t)], tiles(ps[:, QK_T]),
                                     ACT.Copy).then_inc(qk_out, 1)

            with act.Fori(0, 2) as i:
                place = Place(MIX, QKV_STEP, i)
                for part, banks in enumerate((A, B, C)):
                    for o in range(WIDE):
                        round_slab(place, part * WIDE + o + AHEAD)
                        if part > 0 and o in (2, 4):
                            t = o // 2 - 1
                            copy_qk(part - 1, bass.ds(i * CT, CT), t, i * (2 * TT) + ((part - 1) * TT + t))
                        if o == WIDE - 1:
                            evacuate(place, (part + 1) * WIDE, part, banks, bass.ds(i * CH, CH))

            def attend(s, h0):
                if s >= 2:
                    h = h0 + s - 2
                    act.wait_ge(head_out, h + 1)
                    nc.scalar.activation(yT_hi[:, h], ps[:, HEAD_OUT, 0:SEQ], ACT.Copy).then_inc(y_hi, 1)
                if 1 <= s <= HEADS:
                    h = h0 + s - 1
                    act.wait_ge(pt_raw, h + 1)
                    nc.scalar.activation(probsT[:, :], ps[:, PROBS_T, 0:3 * P], ACT.Copy)\
                      .then_inc(pt_copied, 1)
                if s < HEADS:
                    h = h0 + s
                    act.wait_ge(rowmax, (h + 1) * TT)
                    for t, cols in enumerate((slice(0, P), slice(P, 3 * P))):
                        nc.scalar.activation(probs[:, cols], ps[:, SCORES, cols], ACT.Exp,
                                             bias=neg_max[:, t:t + 1],
                                             accum_out=denom[:, t:t + 1]).then_inc(exped, 1)

            place = Place(FOX)
            for c in range(6):
                half, part = divmod(c, 3)
                for o in range(WIDE):
                    e = c * WIDE + o
                    round_slab(place, e + AHEAD)
                    if e == 0:
                        act.wait_ge(forget_landed, 32)
                        nc.scalar.activation(f_hi[:, :, :], f_raw[:, :, :], ACT.Copy).then_inc(f_split, 1)
                    if e == 1:
                        act.wait_ge(f_abs_ready, 1)
                        nc.scalar.activation(f_soft[:, :, :], f_abs[:, :, :], ACT.Exp).then_inc(f_exp, 1)
                        act.wait_ge(f_exp, 1)
                        nc.scalar.activation(f_soft[:, :, :], f_soft[:, :, :], ACT.Ln, bias=1.0)\
                          .then_inc(f_soft_ready, 1)
                    if part > 0 and o in (2, 4):
                        t = o // 2 - 1
                        copy_qk(part - 1, slice(HEADS + half * CT, HEADS + (half + 1) * CT), t,
                                QK_TILES + (half * 2 + part - 1) * TT + t)
                    if e in DIL_SLOTS:
                        attend(DIL_SLOTS[e], 0)
                    if o == WIDE - 1:
                        evacuate(place, e + 1, part, A if c % 2 == 0 else B,
                                 slice(D_MIX + half * CH, D_MIX + (half + 1) * CH))

            def sigmoids(g, count):
                for t in range(TT):
                    act.wait_ge(gate_pre, count + t + 1)
                    nc.scalar.activation(gate_buf[:, g, t], gate_buf[:, g, t], ACT.Sigmoid)\
                      .then_inc(gate_done, 1)

            place = Place(MERGE)
            for e in range(MERGE_FIRST):
                round_slab(place, e + AHEAD)
                if e in FOX_SLOTS:
                    attend(FOX_SLOTS[e], HEADS)
                if e in (WIDE - 1, 2 * WIDE - 1):
                    sigmoids(e // WIDE, e // WIDE * TT)
            with act.Fori(0, NN - 1) as i:
                place = Place(MERGE + MERGE_FIRST, MERGE_STEP, i)
                for o in range(MERGE_STEP):
                    round_slab(place, o + AHEAD)
                    if o == WIDE - 1:
                        round_hidden(i * TT + HID["mix"])
                    if o in (WIDE - 1, 2 * WIDE - 1):
                        sigmoids(o // WIDE, i * (2 * TT) + (2 + o // WIDE) * TT)
            round_hidden(HID["mix"] + (NN - 1) * TT)
            last_down(MERGE_LAST, 2)
            ffn(1, FFN2, 2)
            take_root(3)

        @block.vector
        def _(dve):
            chain = [0]

            def link(done):
                chain[0] += 1
                done.then_inc(small, 1)
                dve.wait_ge(small, chain[0])

            def split_slab(place, offset):
                n = place.start + offset
                if n >= TOTAL:
                    return
                dve.wait_ge(hi_ready, place.slab(offset + 1))
                nc.vector.tensor_tensor(w_lo[:, n % SLOTS], raw[:, n // 2 % LOADS, n % 2 * 2:n % 2 * 2 + 2, :],
                                        w_hi[:, n % SLOTS].bitcast(F32), ALU.subtract).then_inc(lo_ready, 1)

            def scale_x(b, n):
                for t in range(TT):
                    dve.wait_ge(xt_raw, (b * NN + n) * TT + t + 1)
                    if n > 0:
                        dve.wait_ge(xt_lo, (b * NN + n - 1) * TT + t + 1)
                    gain = gains[:, b * KT + n * CT:b * KT + (n + 1) * CT]
                    nc.vector.tensor_tensor(tiles(hidden[:, t]), tiles(ps[:, T + t]),
                                            gain.unsqueeze(2).broadcast_to([P, CT, P]),
                                            ALU.mult).then_inc(xt_scaled, 1)
                for t in range(TT):
                    dve.wait_ge(xt_hi, (b * NN + n) * TT + t + 1)
                    at = xT_hi[:, n * CT:(n + 1) * CT, tokens(t)]
                    nc.vector.tensor_tensor(xT_lo[:, n * CT:(n + 1) * CT, tokens(t)], tiles(hidden[:, t]),
                                            at.bitcast(F32), ALU.subtract).then_inc(xt_lo, 1)

            def take_mean(b):
                dve.wait_ge(squared, (b + 1) * NN * TT)
                link(nc.vector.tensor_reduce(mean[:, :], squares[:, :, :], AXIS_X, ALU.add))
                nc.vector.tensor_scalar(mean[:, :], mean[:, :], 1.0 / D_MODEL, EPS, ALU.mult, ALU.add)\
                  .then_inc(mean_ready, 1)

            def take_rstd(b):
                dve.wait_ge(root_ready, b + 1)
                link(nc.vector.reciprocal(root[:, :], root[:, :]))
                link(nc.vector.tensor_tensor(newton[:, :], root[:, :], root[:, :], ALU.mult))
                link(nc.vector.tensor_tensor(newton[:, :], newton[:, :], mean[:, :], ALU.mult))
                link(nc.vector.tensor_scalar(newton[:, :], newton[:, :], -0.5, 1.5, ALU.mult, ALU.add))
                link(nc.vector.tensor_tensor(rstd[:, :], newton[:, :], root[:, :], ALU.mult))
                nc.vector.tensor_scalar(rstd_q[:, :], rstd[:, :], SCALE, None, ALU.mult)\
                  .then_inc(rstd_ready, 1)

            def split_hidden(count):
                for t in range(TT):
                    dve.wait_ge(ht_hi, count + t + 1)
                    nc.vector.tensor_tensor(hT_lo[:, :, tokens(t)], tiles(ps[:, T + t]),
                                            hT_hi[:, :, tokens(t)].bitcast(F32), ALU.subtract)\
                      .then_inc(ht_lo, 1)

            def multiply_up(place, offset, silu_count):
                dve.wait_ge(slab_done, place.slab(offset))
                for t in range(TT):
                    dve.wait_ge(silu_done, silu_count + t + 1)
                    nc.vector.scalar_tensor_tensor(hidden[:, t], ps[:, B + t], rstd[:, t:t + 1],
                                                   chunk_buf[:, t], ALU.mult, ALU.mult)\
                      .then_inc(hidden_ready, 1)

            def add_down(place, offset, n, factor):
                dve.wait_ge(slab_done, place.slab(offset))
                for t in range(TT):
                    nc.vector.scalar_tensor_tensor(xres[:, t, chunk(n)], ps[:, down_banks(n) + t], factor,
                                                   xres[:, t, chunk(n)], ALU.mult, ALU.add)\
                      .then_inc(added, 1)

            def last_down(start, b, factor):
                place = Place(start)
                for o in range(DOWN):
                    split_slab(place, o + AHEAD)
                    if o % 2 == 1:
                        add_down(place, o + 1, o // 2, factor)
                        if b < 3 and o > 1:
                            scale_x(b, o // 2 - 1)

            def ffn(f, start, b):
                first = Place(start)
                silu = f * FF_CHUNKS * TT
                for o in range(2 * WIDE):
                    split_slab(first, o + AHEAD)
                    if o == 1:
                        scale_x(b, NN - 1)
                    if o == NN:
                        take_mean(b)
                        take_rstd(b)
                    if o == 2 * WIDE - 1:
                        multiply_up(first, o + 1, silu)
                with dve.Fori(0, FF_CHUNKS - 1) as i:
                    place = Place(start + 2 * WIDE, FFN_STEP, i)
                    for o in range(FFN_STEP):
                        split_slab(place, o + AHEAD)
                        if o == WIDE - 1:
                            split_hidden(i * TT + HID[f])
                        if o == 2 * WIDE - 1:
                            multiply_up(place, o + 1, i * TT + (silu + TT))
                        if o > 2 * WIDE and o % 2 == 1:
                            add_down(place, o + 1, (o - 2 * WIDE) // 2, 0.5)
                split_hidden(HID[f] + (FF_CHUNKS - 1) * TT)
                last_down(start + FFN_SLABS - DOWN, b + 1, 0.5)

            dve.wait_ge(gains_raw, 1)
            nc.vector.tensor_copy(gains[:, :], ps[:, T, 0:3 * KT]).then_inc(gains_ready, 1)
            dve.wait_ge(gains_ready, 1)
            for n in range(NN - 1):
                scale_x(0, n)
            for o in range(AHEAD):
                split_slab(Place(0), o)
            nc.vector.tensor_copy(ident_b[:, :], ident).then_inc(consts_ready, 1)
            nc.vector.tensor_copy(tri_b[:, :], tab[:, C_TRI:C_TRI + P]).then_inc(consts_ready, 1)
            ffn(0, 0, 0)
            scale_x(1, NN - 1)
            take_mean(1)
            take_rstd(1)

            def rotate(count, turn):
                dve.wait_ge(evac, count)
                heads = chunk_buf[:, :, :].rearrange("p t (h c) -> p t h c", c=P)
                both = heads[:, :, :, 0:ROPE_DIM]
                shape = [P, TT, CT, ROPE_DIM]
                cos, sin = (tab[:, c:c + TT * ROPE_DIM].rearrange("p (t c) -> p t c", t=TT).unsqueeze(2)
                            .broadcast_to(shape) for c in (C_COS, C_SIN))
                nc.vector.tensor_tensor(rope_a[:, :, :, :], both, cos, ALU.mult).then_inc(turned, 1)
                nc.vector.tensor_tensor(rope_b[:, :, :, :], both, sin, ALU.mult).then_inc(turned, 1)
                dve.wait_ge(turned, turn)
                nc.vector.tensor_tensor(heads[:, :, :, 0:HALF], rope_a[:, :, :, 0:HALF],
                                        rope_b[:, :, :, HALF:ROPE_DIM], ALU.add).then_inc(rotated, 1)
                nc.vector.tensor_tensor(heads[:, :, :, HALF:ROPE_DIM], rope_a[:, :, :, HALF:ROPE_DIM],
                                        rope_b[:, :, :, 0:HALF], ALU.add).then_inc(rotated, 1)

            with dve.Fori(0, 2) as i:
                place = Place(MIX, QKV_STEP, i)
                for o in range(QKV_STEP):
                    split_slab(place, o + AHEAD)
                    if o in (WIDE - 1, 2 * WIDE - 1):
                        part = o // WIDE
                        rotate(i * (3 * TT) + (part + 1) * TT, i * 4 + (part + 1) * 2)

            def attend(s, h0):
                if s >= 2:
                    h = h0 + s - 2
                    dve.wait_ge(y_hi, h + 1)
                    nc.vector.tensor_tensor(yT_lo[:, h], ps[:, HEAD_OUT, 0:SEQ], yT_hi[:, h].bitcast(F32),
                                            ALU.subtract).then_inc(y_lo, 1)
                if s < HEADS:
                    h = h0 + s
                    dve.wait_ge(scores, h + 1)
                    for t, cols in enumerate((slice(0, P), slice(P, 3 * P))):
                        nc.vector.tensor_reduce(neg_max[:, t:t + 1], ps[:, SCORES, cols], AXIS_X,
                                                ALU.max, negate=True).then_inc(rowmax, 1)

            def normalise(h):
                dve.wait_ge(exped, (h + 1) * TT)
                link(nc.vector.reciprocal(inv_denom[:, :], denom[:, :]))
                for t, cols in enumerate((slice(0, P), slice(P, 3 * P))):
                    nc.vector.tensor_scalar(probs[:, cols], probs[:, cols], inv_denom[:, t:t + 1], None,
                                            ALU.mult).then_inc(normed, 1)

            place = Place(FOX)
            for e in range(2 * QKV_STEP):
                split_slab(place, e + AHEAD)
                if e == 0:
                    dve.wait_ge(f_split, 1)
                    nc.vector.tensor_tensor(f_lo[:, :, :], f_raw[:, :, :], f_hi[:, :, :].bitcast(F32),
                                            ALU.subtract).then_inc(f_split_lo, 1)
                if e == 1:
                    for t in range(TT):
                        dve.wait_ge(f_done, t + 1)
                        nc.vector.scalar_tensor_tensor(f_z[:, t], ps[:, C + t, 0:HEADS], rstd[:, t:t + 1],
                                                       f_bias[:, :], ALU.mult, ALU.add).then_inc(f_z_ready, 1)
                    dve.wait_ge(f_z_ready, TT)
                    nc.vector.scalar_tensor_tensor(f_abs[:, :, :], f_z[:, :, :], -1.0, f_z[:, :, :],
                                                   ALU.mult, ALU.min).then_inc(f_abs_ready, 1)
                if e == 2:
                    dve.wait_ge(f_soft_ready, 1)
                    link(nc.vector.tensor_scalar(f_abs[:, :, :], f_z[:, :, :], -1.0, 0.0, ALU.mult, ALU.max))
                    nc.vector.tensor_tensor(f_neg[:, :, :], f_abs[:, :, :], f_soft[:, :, :], ALU.add)\
                      .then_inc(f_ready, 1)
                if e in DIL_SLOTS:
                    attend(DIL_SLOTS[e], 0)
                if e - 1 in DIL_SLOTS and DIL_SLOTS[e - 1] < HEADS:
                    normalise(DIL_SLOTS[e - 1])

            def gate_logits(place, offset, g, banks, landed):
                dve.wait_ge(gate_bias_landed, landed)
                dve.wait_ge(slab_done, place.slab(offset))
                for t in range(TT):
                    nc.vector.scalar_tensor_tensor(gate_buf[:, g, t], ps[:, banks + t], rstd[:, t:t + 1],
                                                   gate_bias[:, g], ALU.mult, ALU.add).then_inc(gate_pre, 1)

            def gate_projection(place, offset, g, banks, count):
                dve.wait_ge(slab_done, place.slab(offset))
                dve.wait_ge(gate_done, count)
                for t in range(TT):
                    dst = hidden[:, t] if g == 0 else gate_buf[:, 1, t]
                    nc.vector.tensor_tensor(dst, ps[:, banks + t], gate_buf[:, g, t], ALU.mult)\
                      .then_inc(gated, 1)
                if g == 1:
                    dve.wait_ge(gated, count)
                    for t in range(TT):
                        nc.vector.tensor_tensor(hidden[:, t], hidden[:, t], gate_buf[:, 1, t], ALU.add)\
                          .then_inc(hidden_ready, 1)

            place = Place(MERGE)
            for e in range(MERGE_FIRST):
                split_slab(place, e + AHEAD)
                if e in FOX_SLOTS:
                    attend(FOX_SLOTS[e], HEADS)
                if e - 1 in FOX_SLOTS and FOX_SLOTS[e - 1] < HEADS:
                    normalise(HEADS + FOX_SLOTS[e - 1])
                if e == WIDE - 1:
                    gate_logits(place, e + 1, 0, A, 32)
                if e == 2 * WIDE - 1:
                    gate_logits(place, e + 1, 1, B, 32)
                if e == 2 * WIDE + HALF_W - 1:
                    gate_projection(place, e + 1, 0, A, TT)
                if e == 2 * WIDE + 2 * HALF_W - 1:
                    gate_projection(place, e + 1, 1, B, 2 * TT)
            with dve.Fori(0, NN - 1) as i:
                place = Place(MERGE + MERGE_FIRST, MERGE_STEP, i)
                for o in range(MERGE_STEP):
                    split_slab(place, o + AHEAD)
                    if o == WIDE - 1:
                        gate_logits(place, o + 1, 0, A, i * 32 + 64)
                        split_hidden(i * TT + HID["mix"])
                    if o == 2 * WIDE - 1:
                        gate_logits(place, o + 1, 1, B, i * 32 + 64)
                    if o == 2 * WIDE + HALF_W - 1:
                        gate_projection(place, o + 1, 0, A, i * (2 * TT) + 3 * TT)
                    if o == 2 * WIDE + 2 * HALF_W - 1:
                        gate_projection(place, o + 1, 1, B, i * (2 * TT) + 4 * TT)
                    if o > MERGE_FIRST and o % 2 == 1:
                        add_down(place, o + 1, (o - MERGE_FIRST) // 2, 1.0)
            split_hidden(HID["mix"] + (NN - 1) * TT)
            last_down(MERGE_LAST, 2, 1.0)
            ffn(1, FFN2, 2)

            take_mean(3)
            take_rstd(3)
            dve.wait_ge(rstd_ready, 4)
            dve.wait_ge(final_gain_landed, 16)
            for n in range(NN):
                for t in range(TT):
                    nc.vector.scalar_tensor_tensor(xres[:, t, chunk(n)], xres[:, t, chunk(n)],
                                                   rstd[:, t:t + 1], final_gain[:, chunk(n)],
                                                   ALU.mult, ALU.mult).then_inc(out_ready, 1)


_INS = ["x", "ffn1_norm", "ffn1_w_gate", "ffn1_w_up", "ffn1_w_down", "mix_norm", "w_in", "b_forget",
        "b_gate_dil", "b_gate_fox", "w_proj_dil", "w_proj_fox", "w_out", "ffn2_norm", "ffn2_w_gate",
        "ffn2_w_up", "ffn2_w_down", "final_norm"]


def kernel(**inputs):
    import concourse.bacc as bacc
    from concourse.bass_utils import run_bass_kernel_spmd

    nc = bacc.Bacc("TRN2", target_bir_lowering=False, num_devices=1)
    arrays, args = {}, []
    for name in _INS:
        a = np.ascontiguousarray(inputs[name])
        arrays[f"in_{name}"] = a
        args.append(nc.dram_tensor(f"in_{name}", a.shape, mybir.dt.from_np(a.dtype),
                                   kind="ExternalInput").ap())
    args.append(nc.dram_tensor("out_y", (1, SEQ, D_MODEL), F32, kind="ExternalOutput").ap())
    build(nc, *args)
    r = run_bass_kernel_spmd(nc, [arrays], core_ids=[0])
    return r.results[0]["out_y"]
```

```python
import numpy as np

import concourse.bass as bass
from concourse import mybir

F32 = mybir.dt.float32
F32R = mybir.dt.float32r
BF16 = mybir.dt.bfloat16
ALU = mybir.AluOpType
ACT = mybir.ActivationFunctionType
AXIS_X = mybir.AxisListType.X

P = 128
SEQ = 256
TT = SEQ // P
D_MODEL = 2048
D_FF = 5632
HEADS = 8
D_MIX = HEADS * P
ROPE_DIM = P // 4
HALF = ROPE_DIM // 2
ROPE_THETA = 500000.0
PATTERNS = ((128, 1), (512, 4), (2048, 16))
EPS = 1e-6
SCALE = float(P) ** -0.5
MASKED = -1e30

CH = 512
KT = D_MODEL // P
CT = CH // P
NN = D_MODEL // CH
FF_CHUNKS = D_FF // CH
F_COL = 6 * D_MIX
G_COL = F_COL + HEADS

SLOTS = 4
LOADS = 4
AHEAD = SLOTS

WIDE, HALF_W, DOWN = 8, 4, 8
FFN_STEP = 2 * WIDE + DOWN
FFN_SLABS = FF_CHUNKS * FFN_STEP
MIX = FFN_SLABS
QKV_STEP = 3 * WIDE
FOX = MIX + 2 * QKV_STEP
MERGE = FOX + 2 * QKV_STEP
MERGE_FIRST = 2 * WIDE + 2 * HALF_W
MERGE_STEP = MERGE_FIRST + DOWN
MERGE_LAST = MERGE + MERGE_FIRST + (NN - 1) * MERGE_STEP
FFN2 = MERGE_LAST + DOWN
TOTAL = FFN2 + FFN_SLABS

C_ID, C_CUM, C_DIL, C_COS, C_SIN, C_TRI, C_END = 0, 128, 384, 640, 704, 768, 896


def constants():
    c = np.zeros((P, C_END), np.float32)
    p = np.arange(P)
    c[:, C_ID:C_ID + P] = np.eye(P)
    c[:, C_CUM:C_CUM + P] = p[:, None] <= p[None, :]
    c[:, C_CUM + P:C_CUM + 2 * P] = 1.0
    gap = P + p[:, None] - np.arange(2 * P)[None, :]
    seen = sum(((gap >= 0) & (gap <= w) & (gap % d == 0)).astype(int) for w, d in PATTERNS)
    c[:, C_DIL:C_DIL + 2 * P] = np.where(seen > 0, np.log(np.maximum(seen, 1)), MASKED)
    inv_freq = np.float32(ROPE_THETA) ** (-np.arange(0, ROPE_DIM, 2, dtype=np.float32) / ROPE_DIM)
    for t in range(TT):
        ang = (t * P + p).astype(np.float32)[:, None] * inv_freq[None, :].astype(np.float32)
        at = t * ROPE_DIM
        c[:, C_COS + at:C_COS + at + ROPE_DIM] = np.tile(np.cos(ang), 2)
        c[:, C_SIN + at:C_SIN + at + ROPE_DIM] = np.concatenate([np.sin(ang), -np.sin(ang)], 1)
    c[:, C_TRI:C_TRI + P] = np.where(p[None, :] <= p[:, None], 0.0, MASKED)
    return c


class Place:

    def __init__(self, start, per=0, i=None):
        assert start % 8 == 0 and per % 8 == 0
        self.start, self.per, self.i = start, per, i

    def slab(self, offset):
        n = self.start + offset
        return n if self.i is None else self.i * self.per + n

    def turn(self, offset):
        n = (self.start + offset) // 8
        return n if self.i is None else self.i * (self.per // 8) + n


def build(nc, x, ffn1_norm, ffn1_w_gate, ffn1_w_up, ffn1_w_down, mix_norm, w_in, b_forget,
          b_gate_dil, b_gate_fox, w_proj_dil, w_proj_fox, w_out, ffn2_norm, ffn2_w_gate,
          ffn2_w_up, ffn2_w_down, final_norm, out):
    table = nc.inline_tensor(constants(), name="shape_tables").ap()

    def rows(w):
        return w.rearrange("l (a p) n -> (l p) a n", p=P)

    gate_w = (rows(ffn1_w_gate), rows(ffn2_w_gate))
    up_w = (rows(ffn1_w_up), rows(ffn2_w_up))
    down_w = (rows(ffn1_w_down), rows(ffn2_w_down))
    in_w, out_w = rows(w_in), rows(w_out)
    proj_w = (rows(w_proj_dil), rows(w_proj_fox))
    x_rows = x.rearrange("b (t p) n -> (b p) t n", p=P)
    out_rows = out.rearrange("b (t p) n -> (b p) t n", p=P)

    def sb(name, shape, dt=F32):
        return nc.alloc_sbuf_tensor(name, shape, dt)

    xres = sb("xres", [P, TT, D_MODEL])
    xT_hi = sb("xT_hi", [P, KT, SEQ], F32R)
    xT_lo = sb("xT_lo", [P, KT, SEQ], F32R)
    raw = sb("raw", [P, LOADS, CT, CH])
    w_hi = sb("w_hi", [P, SLOTS, 2, CH], F32R)
    w_lo = sb("w_lo", [P, SLOTS, 2, CH], F32R)
    hT_hi = sb("hT_hi", [P, CT, SEQ], F32R)
    hT_lo = sb("hT_lo", [P, CT, SEQ], F32R)
    qT_at = nc.sbuf_base
    qT = sb("qT", [P, 2 * HEADS, SEQ])
    kT_at = nc.sbuf_base
    kT = sb("kT", [P, 2 * HEADS, SEQ])
    assert kT_at - qT_at == nc.sbuf_base - kT_at == 2 * HEADS * SEQ * 4
    yT_hi = nc.alloc_sbuf_tensor_at("yT_hi", [P, 2 * HEADS, SEQ], F32R, offset=qT_at)
    yT_lo = nc.alloc_sbuf_tensor_at("yT_lo", [P, 2 * HEADS, SEQ], F32R, offset=kT_at)
    final_gain = nc.alloc_sbuf_tensor_at("final_gain", [P, D_MODEL], F32, offset=qT_at)
    y_gain = nc.alloc_sbuf_tensor_at("y_gain", [P, TT, D_MODEL], F32, offset=kT_at)
    v_sb = sb("v_sb", [P, TT, 2 * D_MIX])
    chunk_buf = sb("chunk_buf", [P, TT, CH])
    hidden = sb("hidden", [P, TT, CH])
    gate_at = nc.sbuf_base
    gate_buf = sb("gate_buf", [P, 2, TT, CH])
    assert nc.sbuf_base - gate_at == 2 * TT * CH * 4
    last_hi = nc.alloc_sbuf_tensor_at("last_hi", [P, CT, SEQ], F32R, offset=gate_at)
    last_lo = nc.alloc_sbuf_tensor_at("last_lo", [P, CT, SEQ], F32R, offset=gate_at + TT * CH * 4)
    gate_bias = sb("gate_bias", [P, 2, CH])
    probs = sb("probs", [P, 3 * P])
    probsT = sb("probsT", [P, 3 * P])
    tab = sb("tab", [P, C_END])
    ident_r = sb("ident_r", [P, P], F32R)
    cum_r = sb("cum_r", [P, 2 * P], F32R)
    dil_hi = sb("dil_hi", [P, 2 * P], F32R)
    dil_lo = sb("dil_lo", [P, 2 * P], F32R)
    ident_b = sb("ident_b", [P, P], BF16)
    tri_b = sb("tri_b", [P, P], BF16)
    rope_a = sb("rope_a", [P, TT, CT, ROPE_DIM])
    rope_b = sb("rope_b", [P, TT, CT, ROPE_DIM])
    f_raw = sb("f_raw", [P, KT, HEADS])
    f_hi = sb("f_hi", [P, KT, HEADS], F32R)
    f_lo = sb("f_lo", [P, KT, HEADS], F32R)
    f_T = sb("f_T", [HEADS, SEQ])
    f_bias = sb("f_bias", [P, HEADS])
    f_z = sb("f_z", [P, TT, HEADS])
    f_abs = sb("f_abs", [P, TT, HEADS])
    f_soft = sb("f_soft", [P, TT, HEADS])
    f_neg = sb("f_neg", [P, TT, HEADS])
    f_neg_hi = sb("f_neg_hi", [P, TT, HEADS], F32R)
    f_neg_lo = sb("f_neg_lo", [P, TT, HEADS], F32R)
    gain_rows = sb("gain_rows", [3 * KT, P])
    gains = sb("gains", [P, 3 * KT])
    squares = sb("squares", [P, TT, NN])
    mean = sb("mean", [P, TT])
    root = sb("root", [P, TT])
    rstd = sb("rstd", [P, TT])
    rstd_q = sb("rstd_q", [P, TT])
    newton = sb("newton", [P, TT])
    neg_max = sb("neg_max", [P, TT])
    denom = sb("denom", [P, TT])
    inv_denom = sb("inv_denom", [P, TT])

    ps = nc.alloc_psum_tensor("ps", [P, 8, CH], F32)
    A, B, C, T = 0, 2, 4, 6
    SCORES, PROBS_T, QK_T, HEAD_OUT = 4, 5, 6, 7


    ident = tab[:, C_ID:C_ID + P]
    cum = tab[:, C_CUM:C_CUM + 2 * P]
    dil_bias = tab[:, C_DIL:C_DIL + 2 * P]

    def sem(name):
        return nc.alloc_semaphore(name)

    raw_landed = [sem(f"raw_landed{n}") for n in range(LOADS)]
    x_landed = [sem(f"x_landed{n}") for n in range(NN)]
    ident_landed = sem("ident_landed")
    table_landed = sem("table_landed")
    gains_landed = sem("gains_landed")
    forget_landed = sem("forget_landed")
    gate_bias_landed = sem("gate_bias_landed")
    final_gain_landed = sem("final_gain_landed")
    stored = sem("stored")
    hi_ready = sem("hi_ready")
    lo_ready = sem("lo_ready")
    slab_done = sem("slab_done")
    gains_raw = sem("gains_raw")
    gains_ready = sem("gains_ready")
    xt_raw = sem("xt_raw")
    xt_scaled = sem("xt_scaled")
    xt_hi = sem("xt_hi")
    xt_lo = sem("xt_lo")
    squared = sem("squared")
    mean_ready = sem("mean_ready")
    root_ready = sem("root_ready")
    table_ahead = sem("table_ahead")
    rstd_ready = sem("rstd_ready")
    small = sem("small")
    silu_done = sem("silu_done")
    hidden_ready = sem("hidden_ready")
    ht_raw = sem("ht_raw")
    ht_hi = sem("ht_hi")
    ht_lo = sem("ht_lo")
    added = sem("added")
    evac = sem("evac")
    rotated = sem("rotated")
    turned = sem("turned")
    qk_raw = sem("qk_raw")
    qk_out = sem("qk_out")
    f_split = sem("f_split")
    f_split_lo = sem("f_split_lo")
    ft_done = sem("ft_done")
    ft_copied = sem("ft_copied")
    f_done = sem("f_done")
    f_z_ready = sem("f_z_ready")
    f_abs_ready = sem("f_abs_ready")
    f_exp = sem("f_exp")
    f_soft_ready = sem("f_soft_ready")
    f_ready = sem("f_ready")
    f_neg_round = sem("f_neg_round")
    f_neg_split = sem("f_neg_split")
    tables_round = sem("tables_round")
    tables_split = sem("tables_split")
    scores = sem("scores")
    rowmax = sem("rowmax")
    exped = sem("exped")
    normed = sem("normed")
    pt_raw = sem("pt_raw")
    pt_copied = sem("pt_copied")
    head_out = sem("head_out")
    y_hi = sem("y_hi")
    y_lo = sem("y_lo")
    gate_pre = sem("gate_pre")
    gate_done = sem("gate_done")
    gated = sem("gated")
    gained = sem("gained")
    out_ready = [sem(f"out_ready{n}") for n in range(NN)]

    ADDED = {0: 0, "mix": FF_CHUNKS * NN * TT, 1: (FF_CHUNKS + NN) * NN * TT}
    HID = {0: 0, "mix": FF_CHUNKS * TT, 1: (FF_CHUNKS + NN) * TT}

    QK_TILES = 2 * 2 * TT
    QKV_TILES = 3 * 2 * TT

    DIL_SLOTS = {4 + 4 * s: s for s in range(HEADS + 2)}
    FOX_SLOTS = {2 * s: s for s in range(HEADS + 2)}

    block = nc.Block()
    with block:

        @block.sync
        def _(sp):
            sp.dma_start(gain_rows[0:KT, :], ffn1_norm.rearrange("l (k p) -> (l k) p", p=P))\
              .then_inc(gains_landed, 16)

            def load_x(n):
                sp.dma_start(xres[:, :, n * CH:(n + 1) * CH],
                             x_rows[:, :, n * CH:(n + 1) * CH]).then_inc(x_landed[n], 16)

            def load(place, offset, src):
                u = (place.start + offset) // 2
                if place.start + offset >= 2 * LOADS:
                    sp.wait_ge(lo_ready, place.slab(offset - 2 * LOADS + 2))
                sp.dma_start(raw[:, u % LOADS], src).then_inc(raw_landed[u % LOADS], 16)

            def load_wide(place, offset, w, cols, k_tiles=KT):
                for kk in range(k_tiles // CT):
                    load(place, offset + 2 * kk, w[:, CT * kk:CT * (kk + 1), cols])

            def load_down(place, offset, w, k_tile):
                for n in range(NN):
                    load(place, offset + 2 * n, w[:, k_tile, n * CH:(n + 1) * CH])

            def ffn(f, start):
                first = Place(start)
                if f == 0:
                    load_x(0)
                    load_x(1)
                    for kk in range(NN):
                        load(first, 2 * kk, gate_w[0][:, CT * kk:CT * (kk + 1), 0:CH])
                        if kk + 2 < NN:
                            load_x(kk + 2)
                else:
                    load_wide(first, 0, gate_w[f], slice(0, CH))
                load_wide(first, WIDE, up_w[f], slice(0, CH))
                with sp.Fori(0, FF_CHUNKS - 1) as i:
                    place = Place(start + 2 * WIDE, FFN_STEP, i)
                    load_wide(place, 0, gate_w[f], bass.ds(i * CH + CH, CH))
                    load_wide(place, WIDE, up_w[f], bass.ds(i * CH + CH, CH))
                    load_down(place, 2 * WIDE, down_w[f], bass.ds(i * CT, CT))
                load_down(Place(start + FFN_SLABS - DOWN), 0, down_w[f],
                          slice((FF_CHUNKS - 1) * CT, FF_CHUNKS * CT))

            ffn(0, 0)
            with sp.Fori(0, 2) as i:
                place = Place(MIX, QKV_STEP, i)
                for part in range(3):
                    load_wide(place, part * WIDE, in_w, bass.ds(i * CH + part * D_MIX, CH))
            with sp.Fori(0, 2) as i:
                place = Place(FOX, QKV_STEP, i)
                for part in range(3):
                    load_wide(place, part * WIDE, in_w, bass.ds(i * CH + (3 + part) * D_MIX, CH))

            def merge(place, n, cols, proj_cols, gd_cols, gf_cols):
                if n is not None:
                    sp.wait_ge(gate_pre, n * (2 * TT))
                for g, b in enumerate((b_gate_dil, b_gate_fox)):
                    sp.dma_start(gate_bias[:, g, :], b[:, cols].broadcast_to([P, CH]))\
                      .then_inc(gate_bias_landed, 16)
                load_wide(place, 0, in_w, gd_cols)
                load_wide(place, WIDE, in_w, gf_cols)
                load_wide(place, 2 * WIDE, proj_w[0], proj_cols, HEADS)
                load_wide(place, 2 * WIDE + HALF_W, proj_w[1], proj_cols, HEADS)

            merge(Place(MERGE), None, slice(0, CH), slice(0, CH), slice(G_COL, G_COL + CH),
                  slice(G_COL + D_MODEL, G_COL + D_MODEL + CH))
            with sp.Fori(0, NN - 1) as i:
                place = Place(MERGE + MERGE_FIRST, MERGE_STEP, i)
                cols = bass.ds(i * CH + CH, CH)
                merge(place, i + 1, cols, cols, bass.ds(i * CH + (G_COL + CH), CH),
                      bass.ds(i * CH + (G_COL + D_MODEL + CH), CH))
                load_down(place, MERGE_FIRST, out_w, bass.ds(i * CT, CT))
            load_down(Place(MERGE_LAST), 0, out_w, slice((NN - 1) * CT, NN * CT))
            sp.wait_ge(slab_done, MERGE_LAST - DOWN)
            sp.dma_start(final_gain[:, :], final_norm.rearrange("(a n) -> a n", a=1)
                         .broadcast_to([P, D_MODEL])).then_inc(final_gain_landed, 16)
            ffn(1, FFN2)
            for n in range(NN):
                sp.wait_ge(out_ready[n], TT)
                sp.dma_start(out_rows[:, :, n * CH:(n + 1) * CH],
                             y_gain[:, :, n * CH:(n + 1) * CH]).then_inc(stored, 16)
            sp.wait_ge(stored, 16 * NN)

        def tokens(t):
            return slice(t * P, (t + 1) * P)

        def chunk(n):
            return slice(n * CH, (n + 1) * CH)

        def down_banks(n):
            return A if n % 2 == 0 else C

        def tiles(ap):
            return ap.rearrange("p (k c) -> p k c", c=P)

        @block.tensor
        def _(pe):
            def pe_loop(n):
                return nc.Fori(0, n, engines=(mybir.EngineType.PE,), hint_back_edge=True)

            def slab(place, offset, banks, lhs, k0, first, last):
                s = (place.start + offset) % SLOTS
                pe.wait_ge(lo_ready, place.slab(offset + 1))
                for j in range(2):
                    for t in range(TT):
                        hi, lo = lhs(k0 + j, t)
                        acc = ps[:, banks + t, :]
                        nc.tensor.matmul(acc, hi, w_hi[:, s, j], start=first and j == 0, stop=False)
                        nc.tensor.matmul(acc, hi, w_lo[:, s, j], start=False, stop=False)
                        done = nc.tensor.matmul(acc, lo, w_hi[:, s, j], start=False,
                                                stop=last and j == 1)
                done.then_inc(slab_done, 1)

            def of_x(k, t):
                return xT_hi[:, k, tokens(t)], xT_lo[:, k, tokens(t)]

            def of_hidden(k, t):
                return hT_hi[:, k, tokens(t)], hT_lo[:, k, tokens(t)]

            def of_last_hidden(k, t):
                return last_hi[:, k, tokens(t)], last_lo[:, k, tokens(t)]

            def wide(place, offset, banks, o):
                slab(place, offset + o, banks, of_x, 2 * o, o == 0, o == WIDE - 1)

            def wide_all(place, offset, banks):
                for o in range(WIDE):
                    wide(place, offset, banks, o)

            def transpose_x(b, n):
                for t in range(TT):
                    if b == 0:
                        pe.wait_ge(x_landed[n], 16)
                    else:
                        pe.wait_ge(added, (0, ADDED["mix"], ADDED[1])[b] - (NN - n) * TT + t + 1)
                    if n > 0:
                        pe.wait_ge(xt_scaled, (b * NN + n - 1) * TT + t + 1)
                    for k in range(CT):
                        done = nc.tensor.transpose(ps[:, T + t, k * P:(k + 1) * P],
                                                   xres[:, t, n * CH + k * P:n * CH + (k + 1) * P], ident)
                    done.then_inc(xt_raw, 1)

            def wide_at_boundary(place, b, banks):
                for o in range(WIDE):
                    if o % 2 == 0:
                        pe.wait_ge(xt_lo, (b * NN + o // 2 + 1) * TT)
                    wide(place, 0, banks, o)
                    if b == 0 and o in (1, 3):
                        transpose_x(0, (o + 3) // 2)
                    if b > 0 and o == 1:
                        transpose_x(b, NN - 1)

            def transpose_hidden(count):
                for t in range(TT):
                    pe.wait_ge(hidden_ready, count + t + 1)
                    for k in range(CT):
                        done = nc.tensor.transpose(ps[:, T + t, k * P:(k + 1) * P],
                                                   hidden[:, t, k * P:(k + 1) * P], ident)
                    done.then_inc(ht_raw, 1)

            def down(place, offset, count, base, next_too=False):
                pe.wait_ge(ht_lo, count + TT)
                for n in range(NN):
                    if n >= 2:
                        pe.wait_ge(added, base + (n - 1) * TT)
                    for o in range(2):
                        slab(place, offset + 2 * n + o, down_banks(n), of_hidden, 2 * o, o == 0, o == 1)
                    if next_too and n == 1:
                        transpose_hidden(count + TT)

            def last_down(start, count, base, boundary):
                place = Place(start)
                pe.wait_ge(ht_lo, count + TT)
                for n in range(NN):
                    if n > 0:
                        pe.wait_ge(added, base + (n - 1) * TT)
                    for o in range(2):
                        slab(place, 2 * n + o, down_banks(n), of_last_hidden, 2 * o, o == 0, o == 1)
                    if boundary is not None and n > 0:
                        transpose_x(boundary, n - 1)

            def ffn(f, start, b):
                silu = f * FF_CHUNKS * TT

                def iteration(place, i, last):
                    hid, base = i * TT + HID[f], i * (NN * TT) + ADDED[f]
                    pe.wait_ge(silu_done, i * TT + (silu + TT))
                    wide_all(place, 0, A)
                    transpose_hidden(hid)
                    wide_all(place, WIDE, B)
                    pe.wait_ge(silu_done, i * TT + (silu + 2 * TT))
                    down(place, 2 * WIDE, hid, base, next_too=last)
                    pe.wait_ge(added, base + (NN - 1) * TT)

                first = Place(start)
                wide_at_boundary(first, b, A)
                wide_all(first, WIDE, B)
                with pe_loop(FF_CHUNKS - 2) as i:
                    iteration(Place(start + 2 * WIDE, FFN_STEP, i), i, False)
                iteration(Place(start + FFN_SLABS - DOWN - FFN_STEP), FF_CHUNKS - 2, True)
                last_down(start + FFN_SLABS - DOWN, HID[f] + (FF_CHUNKS - 1) * TT,
                          ADDED[f] + (FF_CHUNKS - 1) * NN * TT, 1 if f == 0 else None)

            def transpose_qk(t, count, from_sem, from_count):
                pe.wait_ge(from_sem, from_count)
                if t > 0:
                    pe.wait_ge(qk_out, count)
                for k in range(CT):
                    done = nc.tensor.transpose(ps[:, QK_T, k * P:(k + 1) * P],
                                               chunk_buf[:, t, k * P:(k + 1) * P], ident)
                done.then_inc(qk_raw, 1)

            def head_scores(h):
                q, k = qT[:, h, :], kT[:, h, :]
                if h == 0:
                    pe.wait_ge(f_z_ready, TT)
                    pe.wait_ge(qk_out, QK_TILES)
                    pe.wait_ge(tables_split, 1)
                if h == HEADS:
                    pe.wait_ge(qk_out, 2 * QK_TILES)
                    pe.wait_ge(f_neg_split, 1)
                if h > 0:
                    pe.wait_ge(exped, h * TT)
                mm = nc.tensor.matmul
                early, late = ps[:, SCORES, 0:P], ps[:, SCORES, P:3 * P]
                diag = ps[:, SCORES, 2 * P:3 * P]
                if h < HEADS:
                    mm(early, q[:, 0:P], k[:, 0:P], start=True, stop=False)
                    mm(early, ident_r[:, :], dil_hi[:, P:2 * P], start=False, stop=False)
                    mm(early, ident_r[:, :], dil_lo[:, P:2 * P], start=False, stop=True)
                    mm(late, q[:, P:2 * P], k, start=True, stop=False)
                    mm(late, ident_r[:, :], dil_hi[:, :], start=False, stop=False)
                    done = mm(late, ident_r[:, :], dil_lo[:, :], start=False, stop=True)
                else:
                    (hi0, lo0), (hi1, lo1) = (
                        [part[:, t, h - HEADS:h - HEADS + 1].broadcast_to([P, P])
                         for part in (f_neg_hi, f_neg_lo)] for t in range(TT))
                    mm(early, q[:, 0:P], k[:, 0:P], start=True, stop=False)
                    mm(early, hi0, cum_r[:, 0:P], start=False, stop=False)
                    mm(early, lo0, cum_r[:, 0:P], start=False, stop=False)
                    mm(early, ident_b[:, :], tri_b[:, :], start=False, stop=True)
                    mm(late, q[:, P:2 * P], k, start=True, stop=False)
                    mm(late, hi0, cum_r[:, :], start=False, stop=False)
                    mm(late, lo0, cum_r[:, :], start=False, stop=False)
                    mm(diag, hi1, cum_r[:, 0:P], start=False, stop=False)
                    mm(diag, lo1, cum_r[:, 0:P], start=False, stop=False)
                    done = mm(diag, ident_b[:, :], tri_b[:, :], start=False, stop=True)
                done.then_inc(scores, 1)

            def head_transpose(h):
                pe.wait_ge(normed, (h + 1) * TT)
                if h > 0:
                    pe.wait_ge(pt_copied, h)
                for part in range(3):
                    done = nc.tensor.transpose(ps[:, PROBS_T, part * P:(part + 1) * P],
                                               probs[:, part * P:(part + 1) * P], ident)
                done.then_inc(pt_raw, 1)

            def head_values(h):
                pe.wait_ge(pt_copied, h + 1)
                if h % HEADS == 0:
                    pe.wait_ge(evac, (h // HEADS + 1) * QKV_TILES)
                if h > 0:
                    pe.wait_ge(y_lo, h)
                nc.tensor.matmul(ps[:, HEAD_OUT, 0:2 * P], v_sb[:, 0, h * P:(h + 1) * P],
                                 probsT[:, 0:2 * P], start=True, stop=False)
                nc.tensor.matmul(ps[:, HEAD_OUT, P:2 * P], v_sb[:, 1, h * P:(h + 1) * P],
                                 probsT[:, 2 * P:3 * P], start=False, stop=True).then_inc(head_out, 1)

            def attend(s, h0):
                if s >= 2:
                    head_values(h0 + s - 2)
                if 1 <= s <= HEADS:
                    head_transpose(h0 + s - 1)
                if s < HEADS:
                    head_scores(h0 + s)

            pe.wait_ge(ident_landed, 16)
            transpose_x(0, 0)
            pe.wait_ge(gains_landed, 48)
            nc.tensor.transpose(ps[:, C, 0:3 * KT], gain_rows[:, :], ident[0:3 * KT, 0:3 * KT])\
              .then_inc(gains_raw, 1)
            transpose_x(0, 1)
            ffn(0, 0, 0)

            pe.wait_ge(f_split_lo, 1)
            for k in range(KT):
                if k % CT == 0:
                    if k == KT - 2 * CT:
                        transpose_x(1, NN - 1)
                    pe.wait_ge(xt_lo, (NN + k // CT + 1) * TT)
                acc = ps[0:HEADS, B, 0:SEQ]
                nc.tensor.matmul(acc, f_hi[:, k], xT_hi[:, k], start=k == 0, stop=False)
                nc.tensor.matmul(acc, f_lo[:, k], xT_hi[:, k], start=False, stop=False)
                done = nc.tensor.matmul(acc, f_hi[:, k], xT_lo[:, k], start=False, stop=k == KT - 1)
            done.then_inc(ft_done, 1)

            with pe_loop(2) as i:
                place = Place(MIX, QKV_STEP, i)
                for part, banks in enumerate((A, B, C)):
                    if part == 1:
                        pe.wait_ge(ft_copied, 1)
                    for o in range(WIDE):
                        wide(place, part * WIDE, banks, o)
                        if part > 0 and o in (2, 4):
                            t = o // 2 - 1
                            transpose_qk(t, i * (2 * TT) + ((part - 1) * TT + t), rotated, i * 4 + 2 * part)

            place = Place(FOX)
            for c in range(6):
                half, part = divmod(c, 3)
                banks = A if c % 2 == 0 else B
                pe.wait_ge(evac, QKV_TILES + (c - 1) * TT)
                for o in range(WIDE):
                    e = c * WIDE + o
                    wide(place, c * WIDE, banks, o)
                    if e == 1:
                        pe.wait_ge(evac, QKV_TILES)
                        pe.wait_ge(ft_copied, 1)
                        for t in range(TT):
                            nc.tensor.transpose(ps[:, C + t, 0:HEADS], f_T[:, tokens(t)],
                                                ident[0:HEADS, 0:HEADS]).then_inc(f_done, 1)
                    if part > 0 and o in (2, 4):
                        t = o // 2 - 1
                        transpose_qk(t, QK_TILES + (half * 2 + part - 1) * TT + t, evac,
                                     QKV_TILES + c * TT)
                    if e in DIL_SLOTS:
                        attend(DIL_SLOTS[e], 0)

            def project(place, offset, g, banks):
                def of_y(k, t):
                    return yT_hi[:, g * HEADS + k, tokens(t)], yT_lo[:, g * HEADS + k, tokens(t)]

                for o in range(HALF_W):
                    slab(place, offset + o, banks, of_y, 2 * o, o == 0, o == HALF_W - 1)
                    yield o

            place = Place(MERGE)
            e = 0
            for g, banks in enumerate((A, B)):
                pe.wait_ge(evac, 2 * QKV_TILES - (1 - g) * TT)
                for o in range(WIDE):
                    wide(place, g * WIDE, banks, o)
                    if e in FOX_SLOTS:
                        attend(FOX_SLOTS[e], HEADS)
                    e += 1
            for g, banks in enumerate((A, B)):
                pe.wait_ge(gate_pre, (g + 1) * TT)
                pe.wait_ge(y_lo, (g + 1) * HEADS)
                for _ in project(place, 2 * WIDE + g * HALF_W, g, banks):
                    if e in FOX_SLOTS:
                        attend(FOX_SLOTS[e], HEADS)
                    e += 1

            def merge(place, i, last):
                hid, base, used = i * TT + HID["mix"], i * (NN * TT) + ADDED["mix"], i * (2 * TT)
                for g, banks in enumerate((A, B)):
                    pe.wait_ge(gated, used + (g + 1) * TT)
                    wide_all(place, g * WIDE, banks)
                    if g == 0:
                        transpose_hidden(hid)
                for g, banks in enumerate((A, B)):
                    pe.wait_ge(gate_pre, used + (2 + g + 1) * TT)
                    for _ in project(place, 2 * WIDE + g * HALF_W, g, banks):
                        pass
                pe.wait_ge(gated, used + (2 + 1) * TT)
                down(place, MERGE_FIRST, hid, base, next_too=last)
                pe.wait_ge(added, base + (NN - 1) * TT)

            with pe_loop(NN - 2) as i:
                merge(Place(MERGE + MERGE_FIRST, MERGE_STEP, i), i, False)
            merge(Place(MERGE_LAST - MERGE_STEP), NN - 2, True)
            last_down(MERGE_LAST, HID["mix"] + (NN - 1) * TT, ADDED["mix"] + (NN - 1) * NN * TT, 2)
            ffn(1, FFN2, 2)

        @block.scalar
        def _(act):
            act.dma_start(tab[:, 0:P], table[:, 0:P]).then_inc(ident_landed, 16)
            for n, g in ((1, mix_norm), (2, ffn2_norm)):
                act.dma_start(gain_rows[n * KT:(n + 1) * KT, :],
                              g.rearrange("l (k p) -> (l k) p", p=P)).then_inc(gains_landed, 16)

            def round_slab(place, offset):
                n = place.start + offset
                if n >= TOTAL:
                    return
                if n % 2 == 0:
                    act.wait_ge(raw_landed[n // 2 % LOADS], place.turn(offset) * 16 + 16)
                if n >= SLOTS:
                    act.wait_ge(slab_done, place.slab(offset - SLOTS + 1))
                nc.scalar.activation(w_hi[:, n % SLOTS], raw[:, n // 2 % LOADS, n % 2 * 2:n % 2 * 2 + 2, :],
                                     ACT.Copy).then_inc(hi_ready, 1)

            def round_x(b, n):
                for t in range(TT):
                    count = (b * NN + n) * TT + t + 1
                    act.wait_ge(xt_scaled, count)
                    nc.scalar.activation(xT_hi[:, n * CT:(n + 1) * CT, tokens(t)], tiles(hidden[:, t]),
                                         ACT.Copy).then_inc(xt_hi, 1)

            def square(b, n):
                for t in range(TT):
                    if b == 0:
                        act.wait_ge(x_landed[n], 16)
                    else:
                        act.wait_ge(added, (0, ADDED["mix"], ADDED[1], ADDED[1] + ADDED["mix"])[b]
                                    - (NN - n) * TT + t + 1)
                    if n > 0:
                        act.wait_ge(squared, (b * NN + n - 1) * TT + t + 1)
                    nc.scalar.activation(chunk_buf[:, t], xres[:, t, chunk(n)], ACT.Square,
                                         accum_out=squares[:, t, n:n + 1]).then_inc(squared, 1)

            def take_root(b):
                act.wait_ge(mean_ready, b + 1)
                nc.scalar.activation(root[:, :], mean[:, :], ACT.Sqrt).then_inc(root_ready, 1)

            def load_sqrt_table():
                nc.scalar.activation(root[:, :], mean[:, :], ACT.Sqrt).then_inc(table_ahead, 1)

            def round_hidden(count, dst=hT_hi):
                for t in range(TT):
                    act.wait_ge(ht_raw, count + t + 1)
                    nc.scalar.activation(dst[:, :, tokens(t)], tiles(ps[:, T + t]), ACT.Copy)\
                      .then_inc(ht_hi, 1)

            def silu(place, offset, b, used):
                act.wait_ge(rstd_ready, b + 1)
                act.wait_ge(slab_done, place.slab(offset))
                if used is not None:
                    act.wait_ge(hidden_ready, used)
                for t in range(TT):
                    nc.scalar.activation(chunk_buf[:, t], ps[:, A + t], ACT.Silu,
                                         scale=rstd[:, t:t + 1]).then_inc(silu_done, 1)

            def last_down(start, b):
                place = Place(start)
                load_sqrt_table()
                for o in range(DOWN):
                    if o < DOWN - 2:
                        round_slab(place, o + AHEAD)
                    if b < 3 and o % 2 == 1 and o > 1:
                        round_x(b, o // 2 - 1)
                    if b == 1 and o == DOWN - 1:
                        round_x(1, NN - 1)
                    if o % 2 == 1:
                        square(b, o // 2)
                round_slab(place, DOWN - 2 + AHEAD)
                round_slab(place, DOWN - 1 + AHEAD)

            def ffn(f, start, b):
                first = Place(start)
                for o in range(2 * WIDE):
                    round_slab(first, o + AHEAD)
                    if b == 0 and o in (1, 3):
                        round_x(0, (o + 3) // 2)
                    if b > 0 and o == 1:
                        round_x(b, NN - 1)
                    if b == 0 and o < NN:
                        square(0, o)
                    if b == 0 and o == 2 * WIDE - 1:
                        act.wait_ge(forget_landed, 32)
                        nc.scalar.activation(f_hi[:, :, :], f_raw[:, :, :], ACT.Copy).then_inc(f_split, 1)
                    if o == NN:
                        take_root(b)
                    if o == WIDE - 1:
                        silu(first, WIDE, b, None)

                def iteration(place, i, last):
                    for o in range(FFN_STEP):
                        round_slab(place, o + AHEAD)
                        if o == WIDE - 1:
                            silu(place, WIDE, b, i * TT + (HID[f] + TT))
                            round_hidden(i * TT + HID[f])
                        if last and o == 2 * WIDE + 3:
                            round_hidden(i * TT + HID[f] + TT, last_hi)

                with act.Fori(0, FF_CHUNKS - 2) as i:
                    iteration(Place(start + 2 * WIDE, FFN_STEP, i), i, False)
                iteration(Place(start + FFN_SLABS - DOWN - FFN_STEP), FF_CHUNKS - 2, True)
                last_down(start + FFN_SLABS - DOWN, b + 1)

            round_x(0, 0)
            round_x(0, 1)
            for o in range(AHEAD):
                round_slab(Place(0), o)
            act.dma_start(tab[:, P:C_END], table[:, P:C_END]).then_inc(table_landed, 16)
            act.dma_start(f_raw[:, :, :], in_w[:, :, F_COL:G_COL]).then_inc(forget_landed, 16)
            act.dma_start(f_bias[:, :], b_forget.broadcast_to([P, HEADS])).then_inc(forget_landed, 16)
            ffn(0, 0, 0)
            take_root(1)

            def evacuate(place, offset, part, banks, v_cols):
                act.wait_ge(rstd_ready, 2)
                act.wait_ge(slab_done, place.slab(offset))
                for t in range(TT):
                    dst = chunk_buf[:, t] if part < 2 else v_sb[:, t, v_cols]
                    factor = (rstd_q if part == 0 else rstd)[:, t:t + 1]
                    nc.scalar.activation(dst, ps[:, banks + t], ACT.Copy, scale=factor)\
                      .then_inc(evac, 1)

            def copy_qk(part, heads, t, count):
                act.wait_ge(qk_raw, count + 1)
                nc.scalar.activation((qT, kT)[part][:, heads, tokens(t)], tiles(ps[:, QK_T]),
                                     ACT.Copy).then_inc(qk_out, 1)

            with act.Fori(0, 2) as i:
                place = Place(MIX, QKV_STEP, i)
                for part, banks in enumerate((A, B, C)):
                    for o in range(WIDE):
                        round_slab(place, part * WIDE + o + AHEAD)
                        if part > 0 and o in (2, 4):
                            t = o // 2 - 1
                            copy_qk(part - 1, bass.ds(i * CT, CT), t, i * (2 * TT) + ((part - 1) * TT + t))
                        if o == WIDE - 1:
                            evacuate(place, (part + 1) * WIDE, part, banks, bass.ds(i * CH, CH))

            def attend(s, h0):
                if s >= 2:
                    h = h0 + s - 2
                    act.wait_ge(head_out, h + 1)
                    nc.scalar.activation(yT_hi[:, h], ps[:, HEAD_OUT, 0:SEQ], ACT.Copy).then_inc(y_hi, 1)
                if 1 <= s <= HEADS:
                    h = h0 + s - 1
                    act.wait_ge(pt_raw, h + 1)
                    nc.scalar.activation(probsT[:, :], ps[:, PROBS_T, 0:3 * P], ACT.Copy)\
                      .then_inc(pt_copied, 1)
                if s < HEADS:
                    h = h0 + s
                    act.wait_ge(rowmax, (h + 1) * TT)
                    for t, cols in enumerate((slice(0, P), slice(P, 3 * P))):
                        nc.scalar.activation(probs[:, cols], ps[:, SCORES, cols], ACT.Exp,
                                             bias=neg_max[:, t:t + 1],
                                             accum_out=denom[:, t:t + 1]).then_inc(exped, 1)

            place = Place(FOX)
            for c in range(6):
                half, part = divmod(c, 3)
                for o in range(WIDE):
                    e = c * WIDE + o
                    round_slab(place, e + AHEAD)
                    if e == 1:
                        act.wait_ge(f_abs_ready, 1)
                        nc.scalar.activation(f_soft[:, :, :], f_abs[:, :, :], ACT.Exp).then_inc(f_exp, 1)
                        act.wait_ge(f_exp, 1)
                        nc.scalar.activation(f_soft[:, :, :], f_soft[:, :, :], ACT.Ln, bias=1.0)\
                          .then_inc(f_soft_ready, 1)
                    if part > 0 and o in (2, 4):
                        t = o // 2 - 1
                        copy_qk(part - 1, slice(HEADS + half * CT, HEADS + (half + 1) * CT), t,
                                QK_TILES + (half * 2 + part - 1) * TT + t)
                    if e in DIL_SLOTS:
                        attend(DIL_SLOTS[e], 0)
                    if o == WIDE - 1:
                        evacuate(place, e + 1, part, A if c % 2 == 0 else B,
                                 slice(D_MIX + half * CH, D_MIX + (half + 1) * CH))

            def sigmoids(g, count):
                for t in range(TT):
                    act.wait_ge(gate_pre, count + t + 1)
                    nc.scalar.activation(gate_buf[:, g, t], gate_buf[:, g, t], ACT.Sigmoid)\
                      .then_inc(gate_done, 1)

            place = Place(MERGE)
            for e in range(MERGE_FIRST):
                if e in FOX_SLOTS:
                    attend(FOX_SLOTS[e], HEADS)
                round_slab(place, e + AHEAD)
                if e in (WIDE - 1, 2 * WIDE - 1):
                    sigmoids(e // WIDE, e // WIDE * TT)

            def merge(place, i, last):
                for o in range(MERGE_STEP):
                    round_slab(place, o + AHEAD)
                    if o == WIDE - 1:
                        round_hidden(i * TT + HID["mix"])
                    if o in (WIDE - 1, 2 * WIDE - 1):
                        sigmoids(o // WIDE, i * (2 * TT) + (2 + o // WIDE) * TT)
                    if last and o == MERGE_FIRST + 3:
                        round_hidden(i * TT + HID["mix"] + TT, last_hi)

            with act.Fori(0, NN - 2) as i:
                merge(Place(MERGE + MERGE_FIRST, MERGE_STEP, i), i, False)
            merge(Place(MERGE_LAST - MERGE_STEP), NN - 2, True)
            last_down(MERGE_LAST, 2)
            ffn(1, FFN2, 2)
            take_root(3)
            act.wait_ge(rstd_ready, 4)
            for n in range(NN):
                act.wait_ge(gained, (n + 1) * TT)
                nc.scalar.activation(y_gain[:, 1, chunk(n)], y_gain[:, 1, chunk(n)], ACT.Copy,
                                     scale=rstd[:, 1:2]).then_inc(out_ready[n], 1)

        @block.vector
        def _(dve):
            chain = [0]

            def link(done):
                chain[0] += 1
                done.then_inc(small, 1)
                dve.wait_ge(small, chain[0])

            def split_slab(place, offset):
                n = place.start + offset
                if n >= TOTAL:
                    return
                dve.wait_ge(hi_ready, place.slab(offset + 1))
                nc.vector.tensor_tensor(w_lo[:, n % SLOTS], raw[:, n // 2 % LOADS, n % 2 * 2:n % 2 * 2 + 2, :],
                                        w_hi[:, n % SLOTS].bitcast(F32), ALU.subtract).then_inc(lo_ready, 1)

            def scale_x(b, n):
                for t in range(TT):
                    dve.wait_ge(xt_raw, (b * NN + n) * TT + t + 1)
                    if n > 0:
                        dve.wait_ge(xt_lo, (b * NN + n - 1) * TT + t + 1)
                    gain = gains[:, b * KT + n * CT:b * KT + (n + 1) * CT]
                    nc.vector.tensor_tensor(tiles(hidden[:, t]), tiles(ps[:, T + t]),
                                            gain.unsqueeze(2).broadcast_to([P, CT, P]),
                                            ALU.mult).then_inc(xt_scaled, 1)
                for t in range(TT):
                    dve.wait_ge(xt_hi, (b * NN + n) * TT + t + 1)
                    at = xT_hi[:, n * CT:(n + 1) * CT, tokens(t)]
                    nc.vector.tensor_tensor(xT_lo[:, n * CT:(n + 1) * CT, tokens(t)], tiles(hidden[:, t]),
                                            at.bitcast(F32), ALU.subtract).then_inc(xt_lo, 1)

            def take_mean(b):
                dve.wait_ge(squared, (b + 1) * NN * TT)
                link(nc.vector.tensor_reduce(mean[:, :], squares[:, :, :], AXIS_X, ALU.add))
                nc.vector.tensor_scalar(mean[:, :], mean[:, :], 1.0 / D_MODEL, EPS, ALU.mult, ALU.add)\
                  .then_inc(mean_ready, 1)

            def take_rstd(b):
                dve.wait_ge(root_ready, b + 1)
                link(nc.vector.reciprocal(root[:, :], root[:, :]))
                link(nc.vector.tensor_tensor(newton[:, :], root[:, :], root[:, :], ALU.mult))
                link(nc.vector.tensor_tensor(newton[:, :], newton[:, :], mean[:, :], ALU.mult))
                link(nc.vector.tensor_scalar(newton[:, :], newton[:, :], -0.5, 1.5, ALU.mult, ALU.add))
                link(nc.vector.tensor_tensor(rstd[:, :], newton[:, :], root[:, :], ALU.mult))
                nc.vector.tensor_scalar(rstd_q[:, :], rstd[:, :], SCALE, None, ALU.mult)\
                  .then_inc(rstd_ready, 1)

            def split_hidden(count, lo=hT_lo, hi=hT_hi):
                dve.wait_ge(hidden_ready, count + TT)
                for t in range(TT):
                    dve.wait_ge(ht_hi, count + t + 1)
                    nc.vector.tensor_tensor(lo[:, :, tokens(t)], tiles(ps[:, T + t]),
                                            hi[:, :, tokens(t)].bitcast(F32), ALU.subtract)\
                      .then_inc(ht_lo, 1)

            def multiply_up(place, offset, silu_count):
                dve.wait_ge(slab_done, place.slab(offset))
                for t in range(TT):
                    dve.wait_ge(silu_done, silu_count + t + 1)
                    nc.vector.scalar_tensor_tensor(hidden[:, t], ps[:, B + t], rstd[:, t:t + 1],
                                                   chunk_buf[:, t], ALU.mult, ALU.mult)\
                      .then_inc(hidden_ready, 1)

            def add_down(place, offset, n, factor):
                dve.wait_ge(slab_done, place.slab(offset))
                for t in range(TT):
                    nc.vector.scalar_tensor_tensor(xres[:, t, chunk(n)], ps[:, down_banks(n) + t], factor,
                                                   xres[:, t, chunk(n)], ALU.mult, ALU.add)\
                      .then_inc(added, 1)

            def last_down(start, b, factor):
                place = Place(start)
                for o in range(DOWN):
                    if o < DOWN - 2:
                        split_slab(place, o + AHEAD)
                    if o % 2 == 1:
                        add_down(place, o + 1, o // 2, factor)
                        if b < 3 and o > 1:
                            scale_x(b, o // 2 - 1)
                        if b == 3:
                            dve.wait_ge(final_gain_landed, 16)
                            for t in range(TT):
                                dve.wait_ge(added, ADDED[1] + ADDED["mix"] - (NN - o // 2) * TT + t + 1)
                                nc.vector.tensor_tensor(y_gain[:, t, chunk(o // 2)], xres[:, t, chunk(o // 2)],
                                                        final_gain[:, chunk(o // 2)], ALU.mult)\
                                  .then_inc(gained, 1)
                if b == 1:
                    scale_x(1, NN - 1)
                split_slab(place, DOWN - 2 + AHEAD)
                split_slab(place, DOWN - 1 + AHEAD)

            def ffn(f, start, b):
                first = Place(start)
                silu = f * FF_CHUNKS * TT
                for o in range(2 * WIDE):
                    split_slab(first, o + AHEAD)
                    if b == 0 and o in (1, 3):
                        scale_x(0, (o + 3) // 2)
                    if b > 0 and o == 1:
                        scale_x(b, NN - 1)
                    if b == 0 and o == 2 * WIDE - 1:
                        dve.wait_ge(f_split, 1)
                        nc.vector.tensor_tensor(f_lo[:, :, :], f_raw[:, :, :], f_hi[:, :, :].bitcast(F32),
                                                ALU.subtract).then_inc(f_split_lo, 1)
                        dve.wait_ge(table_landed, 16)
                        for dst, src in ((dil_hi, dil_bias), (ident_r, ident), (cum_r, cum),
                                         (ident_b, ident), (tri_b, tab[:, C_TRI:C_TRI + P])):
                            nc.vector.tensor_copy(dst[:, :], src).then_inc(tables_round, 1)
                        dve.wait_ge(tables_round, 5)
                        nc.vector.tensor_tensor(dil_lo[:, :], dil_bias, dil_hi[:, :].bitcast(F32),
                                                ALU.subtract).then_inc(tables_split, 1)
                    if o == NN:
                        take_mean(b)
                        take_rstd(b)
                    if o == 2 * WIDE - 1:
                        multiply_up(first, o + 1, silu)

                def iteration(place, i, last):
                    for o in range(FFN_STEP):
                        split_slab(place, o + AHEAD)
                        if o == WIDE - 1:
                            split_hidden(i * TT + HID[f])
                        if o == 2 * WIDE - 1:
                            multiply_up(place, o + 1, i * TT + (silu + TT))
                        if o > 2 * WIDE and o % 2 == 1:
                            add_down(place, o + 1, (o - 2 * WIDE) // 2, 0.5)
                        if last and o == 2 * WIDE + 3:
                            split_hidden(i * TT + HID[f] + TT, last_lo, last_hi)

                with dve.Fori(0, FF_CHUNKS - 2) as i:
                    iteration(Place(start + 2 * WIDE, FFN_STEP, i), i, False)
                iteration(Place(start + FFN_SLABS - DOWN - FFN_STEP), FF_CHUNKS - 2, True)
                last_down(start + FFN_SLABS - DOWN, b + 1, 0.5)

            dve.wait_ge(gains_raw, 1)
            nc.vector.tensor_copy(gains[:, :], ps[:, C, 0:3 * KT]).then_inc(gains_ready, 1)
            dve.wait_ge(gains_ready, 1)
            scale_x(0, 0)
            scale_x(0, 1)
            for o in range(AHEAD):
                split_slab(Place(0), o)
            ffn(0, 0, 0)
            take_mean(1)
            take_rstd(1)
            dve.wait_ge(ft_done, 1)
            nc.vector.tensor_copy(f_T[:, :], ps[0:HEADS, B, 0:SEQ]).then_inc(ft_copied, 1)

            def rotate(count, turn):
                dve.wait_ge(evac, count)
                heads = chunk_buf[:, :, :].rearrange("p t (h c) -> p t h c", c=P)
                both = heads[:, :, :, 0:ROPE_DIM]
                shape = [P, TT, CT, ROPE_DIM]
                cos, sin = (tab[:, c:c + TT * ROPE_DIM].rearrange("p (t c) -> p t c", t=TT).unsqueeze(2)
                            .broadcast_to(shape) for c in (C_COS, C_SIN))
                nc.vector.tensor_tensor(rope_a[:, :, :, :], both, cos, ALU.mult).then_inc(turned, 1)
                nc.vector.tensor_tensor(rope_b[:, :, :, :], both, sin, ALU.mult).then_inc(turned, 1)
                dve.wait_ge(turned, turn)
                nc.vector.tensor_tensor(heads[:, :, :, 0:HALF], rope_a[:, :, :, 0:HALF],
                                        rope_b[:, :, :, HALF:ROPE_DIM], ALU.add).then_inc(rotated, 1)
                nc.vector.tensor_tensor(heads[:, :, :, HALF:ROPE_DIM], rope_a[:, :, :, HALF:ROPE_DIM],
                                        rope_b[:, :, :, 0:HALF], ALU.add).then_inc(rotated, 1)

            with dve.Fori(0, 2) as i:
                place = Place(MIX, QKV_STEP, i)
                for o in range(QKV_STEP):
                    split_slab(place, o + AHEAD)
                    if o in (WIDE - 1, 2 * WIDE - 1):
                        part = o // WIDE
                        rotate(i * (3 * TT) + (part + 1) * TT, i * 4 + (part + 1) * 2)

            def attend(s, h0):
                if s >= 2:
                    h = h0 + s - 2
                    dve.wait_ge(y_hi, h + 1)
                    nc.vector.tensor_tensor(yT_lo[:, h], ps[:, HEAD_OUT, 0:SEQ], yT_hi[:, h].bitcast(F32),
                                            ALU.subtract).then_inc(y_lo, 1)
                if s < HEADS:
                    h = h0 + s
                    dve.wait_ge(scores, h + 1)
                    for t, cols in enumerate((slice(0, P), slice(P, 3 * P))):
                        nc.vector.tensor_reduce(neg_max[:, t:t + 1], ps[:, SCORES, cols], AXIS_X,
                                                ALU.max, negate=True).then_inc(rowmax, 1)

            def normalise(h):
                dve.wait_ge(exped, (h + 1) * TT)
                link(nc.vector.reciprocal(inv_denom[:, :], denom[:, :]))
                for t, cols in enumerate((slice(0, P), slice(P, 3 * P))):
                    nc.vector.tensor_scalar(probs[:, cols], probs[:, cols], inv_denom[:, t:t + 1], None,
                                            ALU.mult).then_inc(normed, 1)

            place = Place(FOX)
            for e in range(2 * QKV_STEP):
                split_slab(place, e + AHEAD)
                if e == 1:
                    for t in range(TT):
                        dve.wait_ge(f_done, t + 1)
                        nc.vector.scalar_tensor_tensor(f_z[:, t], ps[:, C + t, 0:HEADS], rstd[:, t:t + 1],
                                                       f_bias[:, :], ALU.mult, ALU.add).then_inc(f_z_ready, 1)
                    dve.wait_ge(f_z_ready, TT)
                    nc.vector.scalar_tensor_tensor(f_abs[:, :, :], f_z[:, :, :], -1.0, f_z[:, :, :],
                                                   ALU.mult, ALU.min).then_inc(f_abs_ready, 1)
                if e == 2:
                    dve.wait_ge(f_soft_ready, 1)
                    link(nc.vector.tensor_scalar(f_abs[:, :, :], f_z[:, :, :], -1.0, 0.0, ALU.mult, ALU.max))
                    nc.vector.tensor_tensor(f_neg[:, :, :], f_abs[:, :, :], f_soft[:, :, :], ALU.add)\
                      .then_inc(f_ready, 1)
                    dve.wait_ge(f_ready, 1)
                    nc.vector.tensor_copy(f_neg_hi[:, :, :], f_neg[:, :, :]).then_inc(f_neg_round, 1)
                    dve.wait_ge(f_neg_round, 1)
                    nc.vector.tensor_tensor(f_neg_lo[:, :, :], f_neg[:, :, :], f_neg_hi[:, :, :].bitcast(F32),
                                            ALU.subtract).then_inc(f_neg_split, 1)
                if e in DIL_SLOTS:
                    attend(DIL_SLOTS[e], 0)
                if e - 1 in DIL_SLOTS and DIL_SLOTS[e - 1] < HEADS:
                    normalise(DIL_SLOTS[e - 1])

            def gate_logits(place, offset, g, banks, landed):
                dve.wait_ge(gate_bias_landed, landed)
                dve.wait_ge(slab_done, place.slab(offset))
                for t in range(TT):
                    nc.vector.scalar_tensor_tensor(gate_buf[:, g, t], ps[:, banks + t], rstd[:, t:t + 1],
                                                   gate_bias[:, g], ALU.mult, ALU.add).then_inc(gate_pre, 1)

            def gate_projection(place, offset, g, banks, count):
                dve.wait_ge(slab_done, place.slab(offset))
                dve.wait_ge(gate_done, count)
                for t in range(TT):
                    dst = hidden[:, t] if g == 0 else gate_buf[:, 1, t]
                    nc.vector.tensor_tensor(dst, ps[:, banks + t], gate_buf[:, g, t], ALU.mult)\
                      .then_inc(gated, 1)
                if g == 1:
                    dve.wait_ge(gated, count)
                    for t in range(TT):
                        nc.vector.tensor_tensor(hidden[:, t], hidden[:, t], gate_buf[:, 1, t], ALU.add)\
                          .then_inc(hidden_ready, 1)

            place = Place(MERGE)
            for e in range(MERGE_FIRST):
                if e in FOX_SLOTS:
                    attend(FOX_SLOTS[e], HEADS)
                if e - 1 in FOX_SLOTS and FOX_SLOTS[e - 1] < HEADS:
                    normalise(HEADS + FOX_SLOTS[e - 1])
                split_slab(place, e + AHEAD)
                if e == WIDE - 1:
                    gate_logits(place, e + 1, 0, A, 32)
                if e == 2 * WIDE - 1:
                    gate_logits(place, e + 1, 1, B, 32)
                if e == 2 * WIDE + HALF_W - 1:
                    gate_projection(place, e + 1, 0, A, TT)
                if e == 2 * WIDE + 2 * HALF_W - 1:
                    gate_projection(place, e + 1, 1, B, 2 * TT)

            def merge(place, i, last):
                for o in range(MERGE_STEP):
                    split_slab(place, o + AHEAD)
                    if o == WIDE - 1:
                        gate_logits(place, o + 1, 0, A, i * 32 + 64)
                        split_hidden(i * TT + HID["mix"])
                    if o == 2 * WIDE - 1:
                        gate_logits(place, o + 1, 1, B, i * 32 + 64)
                    if o == 2 * WIDE + HALF_W - 1:
                        gate_projection(place, o + 1, 0, A, i * (2 * TT) + 3 * TT)
                    if o == 2 * WIDE + 2 * HALF_W - 1:
                        gate_projection(place, o + 1, 1, B, i * (2 * TT) + 4 * TT)
                    if o > MERGE_FIRST and o % 2 == 1:
                        add_down(place, o + 1, (o - MERGE_FIRST) // 2, 1.0)
                    if last and o == MERGE_FIRST + 3:
                        split_hidden(i * TT + HID["mix"] + TT, last_lo, last_hi)

            with dve.Fori(0, NN - 2) as i:
                merge(Place(MERGE + MERGE_FIRST, MERGE_STEP, i), i, False)
            merge(Place(MERGE_LAST - MERGE_STEP), NN - 2, True)
            last_down(MERGE_LAST, 2, 1.0)
            ffn(1, FFN2, 2)

            take_mean(3)
            take_rstd(3)
            dve.wait_ge(rstd_ready, 4)
            for n in range(NN):
                dve.wait_ge(gained, (n + 1) * TT)
                nc.vector.tensor_scalar(y_gain[:, 0, chunk(n)], y_gain[:, 0, chunk(n)], rstd[:, 0:1],
                                        None, ALU.mult).then_inc(out_ready[n], 1)


_INS = ["x", "ffn1_norm", "ffn1_w_gate", "ffn1_w_up", "ffn1_w_down", "mix_norm", "w_in", "b_forget",
        "b_gate_dil", "b_gate_fox", "w_proj_dil", "w_proj_fox", "w_out", "ffn2_norm", "ffn2_w_gate",
        "ffn2_w_up", "ffn2_w_down", "final_norm"]


def kernel(**inputs):
    import concourse.bacc as bacc
    from concourse.bass_utils import run_bass_kernel_spmd

    nc = bacc.Bacc("TRN2", target_bir_lowering=False, num_devices=1)
    arrays, args = {}, []
    for name in _INS:
        a = np.ascontiguousarray(inputs[name])
        arrays[f"in_{name}"] = a
        args.append(nc.dram_tensor(f"in_{name}", a.shape, mybir.dt.from_np(a.dtype),
                                   kind="ExternalInput").ap())
    args.append(nc.dram_tensor("out_y", (1, SEQ, D_MODEL), F32, kind="ExternalOutput").ap())
    build(nc, *args)
    r = run_bass_kernel_spmd(nc, [arrays], core_ids=[0])
    return r.results[0]["out_y"]
```
